# Optimizing a Trainium2 kernel written in Bass

```python
import math
import jax, jax.numpy as jnp
from jax import lax
import numpy as np

D_MODEL = 2048
BATCH = 1
SEQ = 1024
DEPTH = 1

CHUNK = 64
D_MIX = D_MODEL
EPS = 1e-6

A_WIDTH = D_MIX // 4
A_GROUPS = 4
A_GDIM = A_WIDTH // A_GROUPS
A_BLOCK = 128

B_HEAD_DIM = 64
B_HEADS = (D_MIX // 2) // B_HEAD_DIM
B_KV_HEADS = 4
B_GQA = B_HEADS // B_KV_HEADS
B_WIDTH = B_HEADS * B_HEAD_DIM
B_KV_WIDTH = B_KV_HEADS * B_HEAD_DIM
WINDOW = 128
WIN_CHUNKS = WINDOW // CHUNK
BAND = WIN_CHUNKS * CHUNK

C_WIDTH = D_MIX - A_WIDTH - B_WIDTH
POOL_SIZES = (2, 4, 8, 16)
C_GROUPS = 4
C_GDIM = C_WIDTH // C_GROUPS

REL_BUCKETS = 32
REL_MAX_DIST = 128

IN_SIZES = (A_WIDTH, A_WIDTH, A_WIDTH,
            B_WIDTH, B_KV_WIDTH, B_KV_WIDTH, B_WIDTH,
            C_WIDTH, C_WIDTH)
D_IN = A_WIDTH * 3 + B_WIDTH * 2 + B_KV_WIDTH * 2 + C_WIDTH * 2

kernel_name = "hybrid_gmlp_swa_pool_streaming_encoder"

def _split_points():
    pts, acc = [], 0
    for s in IN_SIZES[:-1]:
        acc += s
        pts.append(acc)
    return pts

def _rmsnorm(x, g):
    x32 = x.astype(jnp.float32)
    y = x32 * lax.rsqrt(jnp.mean(x32 * x32, axis=-1, keepdims=True) + EPS)
    return (y * g.astype(jnp.float32)).astype(x.dtype)

def _layernorm(x, g, b):
    x32 = x.astype(jnp.float32)
    mu = jnp.mean(x32, axis=-1, keepdims=True)
    var = jnp.mean(jnp.square(x32 - mu), axis=-1, keepdims=True)
    y = (x32 - mu) * lax.rsqrt(var + EPS)
    return (y * g.astype(jnp.float32) + b.astype(jnp.float32)).astype(x.dtype)

def _t5_buckets(rel):
    nb = REL_BUCKETS // 2
    ret = (rel > 0).astype(np.int32) * nb
    n = np.abs(rel)
    max_exact = nb // 2
    large = max_exact + (np.log(np.maximum(n, 1).astype(np.float32) / max_exact)
                         / np.float32(math.log(REL_MAX_DIST / max_exact))
                         * (nb - max_exact)).astype(np.int32)
    large = np.minimum(large, nb - 1)
    return (ret + np.where(n < max_exact, n, large)).astype(np.int32)

def _spatial_gating(u, v, ln_g, ln_b, w_s, b_s):
    B, S, _ = u.shape
    u = jax.nn.gelu(u, approximate=False)
    v = _layernorm(jax.nn.gelu(v, approximate=False), ln_g, ln_b)
    v = v.reshape(B, S // A_BLOCK, A_BLOCK, A_GROUPS, A_GDIM)
    pos = np.arange(A_BLOCK) // CHUNK
    mask = jnp.asarray(pos[None, :] <= pos[:, None], dtype=w_s.dtype)
    mixed = jnp.einsum('gij,bnjgd->bnigd', w_s * mask[None], v)
    mixed = mixed + jnp.transpose(b_s)[None, None, :, :, None]
    return u * mixed.reshape(B, S, A_WIDTH)

def _band(t, n_chunks):
    B, S, H, D = t.shape
    pad = (WIN_CHUNKS - 1) * CHUNK
    tp = jnp.pad(t, ((0, 0), (pad, 0), (0, 0), (0, 0)))
    tp = tp.reshape(B, n_chunks + WIN_CHUNKS - 1, CHUNK, H, D)
    return jnp.concatenate([tp[:, i:i + n_chunks] for i in range(WIN_CHUNKS)], axis=2)

def _swa_sink_attention(q, k, v, sinks, rel_bias):
    B, S, _ = q.shape
    nC = S // CHUNK
    qb = q.reshape(B, nC, CHUNK, B_KV_HEADS, B_GQA, B_HEAD_DIM)
    kb = _band(k.reshape(B, S, B_KV_HEADS, B_HEAD_DIM), nC)
    vb = _band(v.reshape(B, S, B_KV_HEADS, B_HEAD_DIM), nC)
    logits = jnp.einsum('bcqkgd,bcjkd->bckgqj', qb, kb).astype(jnp.float32)
    logits = logits * (1.0 / math.sqrt(B_HEAD_DIM))
    qi = np.arange(CHUNK)[:, None]
    kj = np.arange(BAND)[None, :]
    buckets = _t5_buckets(kj - (WIN_CHUNKS - 1) * CHUNK - qi)
    bias = jnp.transpose(rel_bias.astype(jnp.float32)[buckets], (2, 0, 1))
    logits = logits + bias.reshape(B_KV_HEADS, B_GQA, CHUNK, BAND)[None, None]
    key_chunk = jnp.arange(nC)[:, None] - (WIN_CHUNKS - 1) + (jnp.arange(BAND) // CHUNK)[None, :]
    valid = (key_chunk >= 0)[None, :, None, None, None, :]
    logits = jnp.where(valid, logits, jnp.float32(-1e30))
    sink = sinks.astype(jnp.float32).reshape(B_KV_HEADS, B_GQA)[None, None, :, :, None, None]
    m = jnp.maximum(jnp.max(logits, axis=-1, keepdims=True), sink)
    p = jnp.exp(logits - m)
    p = p / (jnp.sum(p, axis=-1, keepdims=True) + jnp.exp(sink - m))
    out = jnp.einsum('bckgqj,bcjkd->bcqkgd', p.astype(v.dtype), vb)
    return out.reshape(B, S, B_WIDTH)

def _multiscale_pool(xc, w_pool, scale):
    B, S, _ = xc.shape
    xg = xc.reshape(B, S, C_GROUPS, C_GDIM).astype(jnp.float32)
    cs = jnp.pad(lax.cumsum(xg, axis=1), ((0, 0), (1, 0), (0, 0), (0, 0)))
    t = jnp.arange(1, S + 1, dtype=jnp.float32)
    outs = []
    for g, w in enumerate(POOL_SIZES):
        c = cs[:, :, g]
        upper = c[:, 1:]
        lower = jnp.pad(c, ((0, 0), (w - 1, 0), (0, 0)))[:, :S]
        cnt = jnp.minimum(t, jnp.float32(w))[None, :, None]
        outs.append((upper - lower) / cnt - xg[:, :, g])
    pooled = jnp.stack(outs, axis=2).astype(xc.dtype)
    y = jnp.einsum('bsgd,gde->bsge', pooled, w_pool).reshape(B, S, C_WIDTH)
    return y * scale

def setup_inputs(seed: int = 0) -> dict:
    key = jax.random.key(seed)
    ks = jax.random.split(key, 13)
    f32 = jnp.float32
    n = lambda k, shape: jax.random.normal(k, shape, dtype=f32)
    return {
        "x": n(ks[0], (BATCH, SEQ, D_MODEL)),
        "norm_g": 1.0 + 0.1 * n(ks[1], (DEPTH, D_MODEL)),
        "w_in": n(ks[2], (DEPTH, D_MODEL, D_IN)) * D_MODEL ** -0.5,
        "a_ln_g": 1.0 + 0.1 * n(ks[3], (DEPTH, A_WIDTH)),
        "a_ln_b": 0.1 * n(ks[4], (DEPTH, A_WIDTH)),
        "a_w_s": n(ks[5], (DEPTH, A_GROUPS, A_BLOCK, A_BLOCK)) * A_BLOCK ** -0.5,
        "a_b_s": 1.0 + 0.1 * n(ks[6], (DEPTH, A_GROUPS, A_BLOCK)),
        "b_sinks": n(ks[7], (DEPTH, B_HEADS)),
        "rel_bias": 0.5 * n(ks[8], (REL_BUCKETS, B_HEADS)),
        "c_w_pool": n(ks[9], (DEPTH, C_GROUPS, C_GDIM, C_GDIM)) * C_GDIM ** -0.5,
        "c_scale": 1.0 + 0.1 * n(ks[10], (DEPTH, C_WIDTH)),
        "w_out": n(ks[11], (DEPTH, D_MIX, D_MODEL)) * D_MIX ** -0.5,
        "final_g": 1.0 + 0.1 * n(ks[12], (D_MODEL,)),
    }

def reference(x, norm_g, w_in, a_ln_g, a_ln_b, a_w_s, a_b_s, b_sinks, rel_bias,
              c_w_pool, c_scale, w_out, final_g):
    pts = _split_points()
    for l in range(DEPTH):
        h = _rmsnorm(x, norm_g[l])
        proj = jnp.einsum('bsd,de->bse', h, w_in[l])
        ua, va, ga, q, k, v, gb, xc, gc = jnp.split(proj, pts, axis=-1)
        ya = _spatial_gating(ua, va, a_ln_g[l], a_ln_b[l], a_w_s[l], a_b_s[l])
        yb = _swa_sink_attention(q, k, v, b_sinks[l], rel_bias)
        yc = _multiscale_pool(xc, c_w_pool[l], c_scale[l])
        mix = jnp.concatenate([ya * jax.nn.silu(ga),
                               yb * jax.nn.silu(gb),
                               yc * jax.nn.silu(gc)], axis=-1)
        x = x + jnp.einsum('bse,ed->bsd', mix, w_out[l])
    return _rmsnorm(x, final_g)


_drawn_inputs = setup_inputs


def setup_inputs(seed=0):
    import zlib

    import numpy as np

    out = dict(_drawn_inputs(seed))
    spreads = {}
    factors = {'a_ln_g': 3.791,
     'a_ln_b': 3.707,
     'a_b_s': 2.991,
     'b_sinks': 33.159,
     'rel_bias': 3.246,
     'c_scale': 2.752}
    for name, (base, spread) in spreads.items():
        noise = np.random.default_rng([zlib.crc32(name.encode()), seed]).standard_normal(out[name].shape)
        drawn = base * np.exp(spread * noise) if base else spread * noise
        out[name] = __import__('jax').numpy.asarray(drawn.astype(out[name].dtype))
    for name, factor in factors.items():
        out[name] = (out[name] * factor).astype(out[name].dtype)
    return out
```

```python
import math
from contextlib import ExitStack

import numpy as np

import concourse.bass as bass
from concourse import mybir

ALU = mybir.AluOpType
ACT = mybir.ActivationFunctionType
AX = mybir.AxisListType
F32 = mybir.dt.float32
F32R = mybir.dt.float32r

P = 128
SEQ, D = 1024, 2048
HALVES = 2
HS = SEQ // HALVES
ST = HS // P
KT = D // P
CHUNK = 64
HEADS, KV_HEADS, DH = 16, 4, 64
EPS = 1e-6
REL_BUCKETS, REL_MAX_DIST = 32, 128
REL = 192
POOLS = (2, 4, 8, 16)
HIST = 16

G_K, G_V, G_VA, G_Q, G_UA, G_GA, G_C, G_OUT, GROUPS = 0, 2, 4, 8, 24, 28, 32, 40, 56
GW = 2048
PIECES = 16
SLOT_S, SLOT_PT, SLOT_PV = 9, 10, 11
GATES = 20
T_TILES = 34
M_A, M_C = 8, 12


def t_index(g):
    return g if g < G_V else g - G_Q + 2


def gate_index(g):
    if g < G_UA:
        return (g - G_Q) // 2
    if g < G_C:
        return 8 + g - G_UA
    return 16 + (g - G_C) // 2


def is_t(g):
    return g < G_V or G_Q <= g < G_OUT


def is_gate(g):
    return (G_Q <= g < G_UA and g % 2 == 1) or G_UA <= g < G_C or (G_C <= g < G_OUT and g % 2 == 1)


def tile_heads(i):
    return 8 * (i // 4) + i % 4, 8 * (i // 4) + 4 + i % 4


def build(nc, x, x_t, w, norm_g, ln_g, ln_b, w_s, b_s, sinks, rel_bias, one_hot, inv_count, w_pool,
          c_scale, final_g, out):
    table = nc.dram_tensor("rel_table", [CHUNK, HEADS, REL], F32).ap()
    with ExitStack() as ctx:
        def sb(name, shape, dt=F32):
            return ctx.enter_context(nc.sbuf_tensor(name, shape, dt))

        def psum(name):
            return ctx.enter_context(nc.psum_tensor(name, [P, 512], F32))

        def sem(name):
            return ctx.enter_context(nc.semaphore(name))

        op_hi = sb("op_hi", [P, KT, HS], F32R)
        op_lo = sb("op_lo", [P, KT, HS], F32R)
        mix = sb("mix", [P, KT, HS])
        raw = sb("raw", [P, 2, GW])
        w_hi = sb("w_hi", [P, 2, GW], F32R)
        w_lo = sb("w_lo", [P, 2, GW], F32R)
        x_raw = sb("x_raw", [P, 2, HS])
        x_sq = sb("x_sq", [P, HS])
        rstd_row = sb("rstd_row", [P, HS])
        k_t = sb("k_t", [P, 2, CHUNK + HS])
        v = sb("v", [P, ST, KV_HEADS * DH])
        v_prev = sb("v_prev", [P, ST, KV_HEADS * DH])
        probs = sb("probs", [P, 528])
        probs_t = sb("probs_t", [P, 528])
        q_t = sb("q_t", [P, 528])
        pre = sb("pre", [P, 528])
        act = sb("act", [P, 528])
        aux = sb("aux", [P, 528])
        norm_g_sb = sb("norm_g_sb", [P, KT])
        ln_g_sb = sb("ln_g_sb", [P, 512])
        ln_b_sb = sb("ln_b_sb", [P, 512])
        w_s_sb = sb("w_s_sb", [P, 4, P])
        b_s_sb = sb("b_s_sb", [P, 4, P])
        sink_sb = sb("sink_sb", [P, HEADS])
        rel_sb = sb("rel_sb", [REL_BUCKETS, HEADS])
        one_hot_sb = sb("one_hot_sb", [REL_BUCKETS, REL])
        table_sb = sb("table_sb", [HEADS, REL])
        bias = sb("bias", [P, HEADS, P])
        inv_sb = sb("inv_sb", [P, 4, HIST])
        w_pool_sb = sb("w_pool_sb", [P, 4, P])
        c_scale_sb = sb("c_scale_sb", [P, 4])
        final_g_sb = sb("final_g_sb", [P, D])
        ones = sb("ones", [P, P])
        ident = sb("ident", [P, P])
        hist = sb("hist", [P, 4, HIST])
        head_sum = sb("head_sum", [P, HIST])
        eps_sb = sb("eps_sb", [P, 1])
        root_row = sb("root_row", [P, 4])
        rstd_col = sb("rstd_col", [P, 4])
        root_ln = sb("root_ln", [P, 4])
        rstd_ln = sb("rstd_ln", [P, 4])
        bn = sb("bn", [P, 4, 6])
        mean_var = sb("mean_var", [P, 4, 2])
        row_max = sb("row_max", [P, 4])
        sink_d = sb("sink_d", [P, 4])
        sink_e = sb("sink_e", [P, 4])
        row_sum = sb("row_sum", [P, 4])
        row_inv = sb("row_inv", [P, 4])
        ssq = sb("ssq", [P, ST, 4])
        ssq_sum = sb("ssq_sum", [P, ST])
        root_y = sb("root_y", [P, ST])
        rstd_y = sb("rstd_y", [P, ST])
        residual = [probs, probs_t, q_t, aux]

        T = [psum(f"t_bank{i}") for i in range(2)]
        N = [psum(f"n_bank{i}") for i in range(4)]
        E = [psum(f"e_bank{i}") for i in range(2)]
        S_bank, PT_bank, O_bank = (N[0], N[3]), N[1], N[2]

        raw_loaded = [sem(f"raw_loaded{i}") for i in range(2)]
        hi_done, lo_done, group_done = sem("hi_done"), sem("lo_done"), sem("group_done")
        norm_g_loaded = sem("norm_g_loaded")
        x_loaded = [sem(f"x_loaded{i}") for i in range(KT // 4)]
        x_raw_loaded = sem("x_raw_loaded")
        x_hi_done, x_lo_done, x_sq_done, x_acc_done = (sem("x_hi_done"), sem("x_lo_done"), sem("x_sq_done"),
                                                       sem("x_acc_done"))
        x_read = sem("x_read")
        m_hi_done, m_lo_done = sem("m_hi_done"), sem("m_lo_done")
        consts_loaded, consts_set = sem("consts_loaded"), sem("consts_set")
        table_done, table_copied, table_stored, bias_loaded = (sem("table_done"), sem("table_copied"),
                                                               sem("table_stored"), sem("bias_loaded"))
        stats_done, root_done, rstd_done = sem("stats_done"), sem("root_done"), sem("rstd_done")
        t_evac, v_evac, v_saved, va_evac = sem("t_evac"), sem("v_evac"), sem("v_saved"), sem("va_evac")
        v_ready = sem("v_ready")
        ln_var, ln_root, ln_done = sem("ln_var"), sem("ln_root"), sem("ln_done")
        s_ready, shifted, exp_done, p_ready = sem("s_ready"), sem("shifted"), sem("exp_done"), sem("p_ready")
        pt_ready, pt_evac, o_ready, o_evac = sem("pt_ready"), sem("pt_evac"), sem("o_ready"), sem("o_evac")
        gate_fn, gate_used = sem("gate_fn"), sem("gate_used")
        sgu_ready, pool_in, pool_ready = sem("sgu_ready"), sem("pool_in"), sem("pool_ready")
        res_loaded = [sem(f"res_loaded{i}") for i in range(ST)]
        y_evac, ssq_done, ssq_summed, y_root, y_normed, y_stored = (sem("y_evac"), sem("ssq_done"), sem("ssq_summed"), sem("y_root"),
                                                        sem("y_normed"), sem("y_stored"))
        dve_settled, act_settled, pool_settled = sem("dve_settled"), sem("act_settled"), sem("pool_settled")

        block = ctx.enter_context(nc.Block())

        @block.sync
        def _(sp):
            def store(sp, half, st):
                sp.wait_ge(y_normed, ST * half + st + 1)
                s0 = HS * half + P * st
                sp.dma_start(out[s0:s0 + P, :], mix[:, 4 * st:4 * st + 4, :].rearrange("p c d -> p (c d)")
                             ).then_inc(y_stored, 16)

            def load_group(G):
                if G >= 2:
                    sp.wait_ge(lo_done, 2 * (G - 1))
                sp.dma_start(raw[:, G % 2, :], w[G % GROUPS]).then_inc(raw_loaded[G % 2], 16)

            sp.dma_start(norm_g_sb[:], norm_g).then_inc(norm_g_loaded, 16)
            for a in range(KT // 4):
                sp.dma_start(mix[:, 4 * a:4 * a + 4, :].rearrange("p k s -> p (k s)"),
                             x_t[0, a]).then_inc(x_loaded[a], 16)
                if a < 2:
                    load_group(a)
            sp.wait_ge(table_copied, 1)
            sp.dma_start(table.rearrange("q h r -> h q r"),
                         table_sb[:].unsqueeze(1).broadcast_to([HEADS, CHUNK, REL])).then_inc(table_stored, 16)
            sp.wait_ge(table_stored, 16)
            for q0, q1, s0, s1, at in ((0, 64, 0, 64, 127), (0, 64, 64, 128, 63), (64, 128, 0, 128, 63)):
                sp.dma_start(bias[q0:q1, :, s0:s1],
                             bass.AP(table.tensor, at, [[HEADS * REL - 1, CHUNK], [REL, HEADS], [1, s1 - s0]])
                             ).then_inc(bias_loaded, 16)

            for half in range(HALVES):
                for g in range(GROUPS):
                    G = GROUPS * half + g
                    if G + 2 < GROUPS * HALVES:
                        load_group(G + 2)
                    if g >= G_OUT and g % 4 == 1:
                        c = (g - G_OUT) // 4
                        n = 4 * half + c
                        if c == 0:
                            sp.wait_ge(m_lo_done, KT * (half + 1))
                        else:
                            sp.wait_ge(y_evac, ST * n)
                        for st in range(ST):
                            s0 = HS * half + P * st
                            sp.dma_start(residual[st][:, 0:512], x[s0:s0 + P, 512 * c:512 * c + 512]
                                         ).then_inc(res_loaded[st], 16)
                    if half == 0 and g >= G_OUT + 12:
                        for a in range(2 * (g - G_OUT - 12), 2 * (g - G_OUT - 12) + 2):
                            if a >= 1:
                                sp.wait_ge(x_lo_done, KT + 2 * a)
                                sp.wait_ge(x_sq_done, KT + 2 * a)
                            sp.dma_start(x_raw[:].rearrange("p k s -> p (k s)"),
                                         x_t[1, a // 2, :, 1024 * (a % 2):1024 * (a % 2) + 1024]
                                         ).then_inc(x_raw_loaded, 16)
                    if half == 1 and 1 <= g <= ST:
                        store(sp, 0, g - 1)
            for st in range(ST):
                store(sp, 1, st)
            sp.wait_ge(y_stored, 16 * ST * HALVES)

        @block.gpsimd
        def _(pool):
            settled = [0]

            def settle(ins):
                settled[0] += 1
                ins.then_inc(pool_settled, 1)
                pool.wait_ge(pool_settled, settled[0])

            pool.memset(ones[:], 1.0).then_inc(consts_set, 1)
            pool.memset(eps_sb[:], EPS).then_inc(consts_set, 1)
            settle(pool.memset(ident[:], 0.0))
            pool.affine_select(out=ident[:], in_=ident[:], compare_op=ALU.not_equal, fill=1.0, base=0,
                               pattern=[[-1, P]], channel_multiplier=1).then_inc(consts_set, 1)

            def rows(a, n):
                return bass.AP(a.tensor, 0, [[0, P], [1, n]])

            for dst, src in ((rel_sb[:], rel_bias), (one_hot_sb[:], one_hot), (sink_sb[:], rows(sinks, HEADS)),
                             (ln_g_sb[:], rows(ln_g, 512)), (ln_b_sb[:], rows(ln_b, 512)),
                             (w_s_sb[:].rearrange("p g i -> p (g i)"), w_s),
                             (b_s_sb[:].rearrange("p g i -> p (g i)"), rows(b_s, 512)),
                             (inv_sb[:].rearrange("p g i -> p (g i)"), rows(inv_count, 4 * HIST)),
                             (w_pool_sb[:].rearrange("p g i -> p (g i)"), w_pool), (c_scale_sb[:], c_scale),
                             (final_g_sb[:], rows(final_g, D))):
                pool.dma_start(dst, src).then_inc(consts_loaded, 16)

            for half in range(HALVES):
                for kt in range(KT):
                    n = KT * half + kt
                    if half == 0:
                        pool.wait_ge(x_loaded[kt // 4], 16)
                        src = mix[:, kt, :]
                    else:
                        pool.wait_ge(x_raw_loaded, 16 * (kt // 2 + 1))
                        src = x_raw[:, kt % 2, :]
                    if kt == 0:
                        if half == 1:
                            pool.wait_ge(t_evac, T_TILES)
                        pool.tensor_tensor(rstd_row[:], src, src, ALU.mult).then_inc(x_sq_done, 1)
                        pool.wait_ge(x_sq_done, n + 1)
                        continue
                    pool.tensor_tensor(x_sq[:], src, src, ALU.mult).then_inc(x_sq_done, 1)
                    pool.wait_ge(x_sq_done, n + 1)
                    pool.tensor_tensor(rstd_row[:], rstd_row[:], x_sq[:], ALU.add).then_inc(x_acc_done, 1)
                    pool.wait_ge(x_acc_done, (KT - 1) * half + kt)

        @block.scalar
        def _(sc):
            def square_y(half, c):
                for st in range(ST):
                    n = ST * (4 * half + c) + st
                    sc.wait_ge(y_evac, n + 1)
                    if n >= 1:
                        sc.wait_ge(ssq_done, n)
                    sc.activation(act[:, 0:512], mix[:, 4 * st + c, :], ACT.Square,
                                  accum_out=ssq[:, st, c:c + 1]).then_inc(ssq_done, 1)

            def root_of_y(half):
                sc.wait_ge(ssq_summed, half + 1)
                sc.activation(root_y[:], ssq_sum[:], ACT.Sqrt, bias=eps_sb[:], scale=1.0 / D
                                     ).then_inc(y_root, 1)

            def split_hi(G):
                slot = G % 2
                sc.wait_ge(raw_loaded[slot], 16 * (G // 2 + 1))
                if G >= 2:
                    sc.wait_ge(group_done, G - 1)
                for s in range(2):
                    sc.activation(w_hi[:, slot, 1024 * s:1024 * s + 1024], raw[:, slot, 1024 * s:1024 * s + 1024],
                                  ACT.Copy).then_inc(hi_done, 1)

            def x_hi(half, kt):
                src = mix[:, kt, :] if half == 0 else x_raw[:, kt % 2, :]
                if half == 0:
                    sc.wait_ge(x_loaded[kt // 4], 16)
                else:
                    sc.wait_ge(x_raw_loaded, 16 * (kt // 2 + 1))
                    sc.wait_ge(group_done, G_OUT + 12 + kt // 4 + 1)
                sc.activation(op_hi[:, kt, :], src, ACT.Copy, scale=norm_g_sb[:, kt:kt + 1]
                              ).then_inc(x_hi_done, 1)

            def mix_hi(half, kt):
                if kt < 12:
                    sc.wait_ge(x_read, 3 * half + kt // 4 + 1)
                else:
                    sc.wait_ge(group_done, GROUPS * half + G_OUT)
                sc.wait_ge(gate_used, GATES * (half + 1) - (1 if kt < KT - 1 else 0))
                sc.activation(op_hi[:, kt, :], mix[:, kt, :], ACT.Copy).then_inc(m_hi_done, 1)

            sc.wait_ge(norm_g_loaded, 16)
            for kt in range(4):
                x_hi(0, kt)
            split_hi(0)
            for kt in range(4, KT):
                x_hi(0, kt)
            sc.wait_ge(consts_set, 3)
            for half in range(HALVES):
                for g in range(GROUPS):
                    G = GROUPS * half + g
                    if G + 1 < GROUPS * HALVES:
                        split_hi(G + 1)
                    if half == 1 and g == 0:
                        for kt in range(12, KT):
                            x_hi(1, kt)
                    if g == 2:
                        sc.wait_ge(stats_done, half + 1)
                        sc.activation(rstd_row[:], E[0][:], ACT.Sqrt, bias=eps_sb[:], scale=1.0 / D
                                      ).then_inc(root_done, 1)
                        sc.activation(root_row[:], E[1][:, 0:4], ACT.Sqrt, bias=eps_sb[:], scale=1.0 / D
                                      ).then_inc(root_done, 1)
                    if g == G_VA:
                        sc.wait_ge(group_done, G)
                        sc.wait_ge(rstd_done, 2 * (half + 1))
                        sc.wait_ge(v_saved, half + 1)
                        for st in range(ST):
                            sc.activation(v[:, st, :], N[st][:, 0:256], ACT.Copy, scale=rstd_col[:, st:st + 1]
                                          ).then_inc(v_evac, 1)
                    if g == G_Q:
                        sc.wait_ge(group_done, G)
                        if half == 1:
                            sc.wait_ge(y_stored, 16 * ST)
                        for st in range(ST):
                            sc.activation(mix[:, M_A:M_A + 4, P * st:P * st + P],
                                          N[st][:].rearrange("p (j d) -> p j d", j=4), ACT.Gelu,
                                          scale=rstd_col[:, st:st + 1]).then_inc(va_evac, 1)
                        sc.wait_ge(ln_var, half + 1)
                        sc.activation(root_ln[:], mean_var[:, :, 1], ACT.Sqrt, bias=eps_sb[:]
                                      ).then_inc(ln_root, 1)
                    if g >= 1 and is_gate(g - 1):
                        n = GATES * half + gate_index(g - 1)
                        sc.wait_ge(t_evac, T_TILES * half + t_index(g - 1) + 1)
                        if n >= 1:
                            sc.wait_ge(gate_used, n)
                        if g - 1 < G_UA:
                            sc.activation(act[:, 0:HS], pre[:, 0:HS], ACT.Exp, scale=-1.0).then_inc(gate_fn, 1)
                        else:
                            sc.activation(act[:, 0:HS], pre[:, 0:HS], ACT.Gelu if g - 1 < G_GA else ACT.Silu
                                          ).then_inc(gate_fn, 1)
                    n = g - 1 - SLOT_PT
                    if 0 <= n < PIECES:
                        m = PIECES * half + n
                        sc.wait_ge(pt_ready, m + 1)
                        if m >= 1:
                            sc.wait_ge(o_ready, m)
                        sc.activation(probs_t[:, 0:512], PT_bank[:], ACT.Copy).then_inc(pt_evac, 1)
                    n = g - 1 - SLOT_S
                    if 0 <= n < PIECES:
                        m = PIECES * half + n
                        sc.wait_ge(shifted, 2 * m + 2)
                        sc.activation(sink_e[:], sink_d[:], ACT.Exp).then_inc(exp_done, 1)
                        sc.activation(probs[:, 0:512], probs[:, 0:512], ACT.Exp).then_inc(exp_done, 1)
                    if g == G_OUT - 1:
                        for kt in range(KT - 1):
                            mix_hi(half, kt)
                    if g == G_OUT:
                        mix_hi(half, KT - 1)
                    if g >= G_OUT + 4 and g % 4 == 0:
                        square_y(half, (g - G_OUT) // 4 - 1)
                    if half == 1 and g == 0:
                        square_y(0, 3)
                        root_of_y(0)
                    if half == 0 and g > G_OUT + 12:
                        for kt in range(4 * (g - G_OUT - 13), 4 * (g - G_OUT - 12)):
                            x_hi(1, kt)
            square_y(1, 3)
            root_of_y(1)

        @block.vector
        def _(ve):
            settled = [0]

            def settle(ins):
                settled[0] += 1
                ins.then_inc(dve_settled, 1)
                ve.wait_ge(dve_settled, settled[0])

            def split_lo(G):
                slot = G % 2
                for s in range(2):
                    ve.wait_ge(hi_done, 2 * G + s + 1)
                    part = slice(1024 * s, 1024 * s + 1024)
                    ve.tensor_tensor(w_lo[:, slot, part], raw[:, slot, part], w_hi[:, slot, part].bitcast(F32),
                                     ALU.subtract).then_inc(lo_done, 1)

            def x_lo(half, kt):
                src = mix[:, kt, :] if half == 0 else x_raw[:, kt % 2, :]
                ve.wait_ge(x_hi_done, KT * half + kt + 1)
                ve.scalar_tensor_tensor(out=op_lo[:, kt, :], in0=src, scalar=norm_g_sb[:, kt:kt + 1],
                                        in1=op_hi[:, kt, :].bitcast(F32), op0=ALU.mult, op1=ALU.subtract
                                        ).then_inc(x_lo_done, 1)

            def mix_lo(half, kt):
                ve.wait_ge(m_hi_done, KT * half + kt + 1)
                ve.tensor_tensor(op_lo[:, kt, :], mix[:, kt, :], op_hi[:, kt, :].bitcast(F32), ALU.subtract
                                 ).then_inc(m_lo_done, 1)

            def take(half, g, dst):
                ve.tensor_tensor(dst, T[t_index(g) % 2][:], rstd_row[:], ALU.mult).then_inc(t_evac, 1)
                ve.wait_ge(t_evac, T_TILES * half + t_index(g) + 1)

            def gate_ready(half, g):
                ve.wait_ge(gate_fn, GATES * half + gate_index(g) + 1)

            def softmax_scores(half, n):
                i, tp, m = n // 2, n % 2, PIECES * half + n
                ve.wait_ge(s_ready, m + 1)
                if m == 0:
                    ve.wait_ge(bias_loaded, 48)
                for a in range(2):
                    settle(ve.scalar_tensor_tensor(
                        out=probs[:, 256 * a:256 * a + 256].rearrange("p (t s) -> p t s", t=2),
                        in0=S_bank[a][:, 0:256].rearrange("p (t s) -> p t s", t=2), scalar=DH ** -0.5,
                        in1=bias[:, 2 * i + a, :].unsqueeze(1).broadcast_to([P, 2, P]),
                        op0=ALU.mult, op1=ALU.add))
                if half == 0 and tp == 0:
                    off = probs[0:64, 0:512].rearrange("p (h t s) -> p h t s", h=2, t=2)[:, :, 0, 64:128]
                    settle(ve.memset(off, -1e30))
                scores = probs[:, 0:512].rearrange("p (b s) -> p b s", b=4)
                sink4 = sink_sb[:, 2 * i:2 * i + 2].unsqueeze(2).broadcast_to([P, 2, 2])
                settle(ve.tensor_reduce(row_max[:], scores, AX.X, ALU.max))
                settle(ve.tensor_tensor(row_max[:].rearrange("p (h t) -> p h t", h=2),
                                        row_max[:].rearrange("p (h t) -> p h t", h=2), sink4, ALU.max))
                ve.tensor_tensor(sink_d[:].rearrange("p (h t) -> p h t", h=2), sink4,
                                 row_max[:].rearrange("p (h t) -> p h t", h=2), ALU.subtract
                                 ).then_inc(shifted, 1)
                ve.tensor_tensor(scores, scores, row_max[:].unsqueeze(2).broadcast_to([P, 4, P]),
                                 ALU.subtract).then_inc(shifted, 1)

            def softmax_norm(half, n):
                m = PIECES * half + n
                ve.wait_ge(exp_done, 2 * m + 2)
                scores = probs[:, 0:512].rearrange("p (b s) -> p b s", b=4)
                settle(ve.tensor_reduce(row_sum[:], scores, AX.X, ALU.add))
                settle(ve.tensor_tensor(row_sum[:], row_sum[:], sink_e[:], ALU.add))
                settle(ve.reciprocal(row_inv[:], row_sum[:]))
                ve.tensor_tensor(scores, scores, row_inv[:].unsqueeze(2).broadcast_to([P, 4, P]),
                                 ALU.mult).then_inc(p_ready, 1)

            def layer_norm(st):
                view = mix[:, M_A:M_A + 4, P * st:P * st + P]
                settle(ve.tensor_scalar(view, view, mean_var[:, st, 0:1], rstd_ln[:, st:st + 1],
                                        ALU.subtract, ALU.mult))
                settle(ve.tensor_tensor(view, view, ln_g_sb[:].rearrange("p (j d) -> p j d", j=4), ALU.mult))
                ve.tensor_tensor(view, view, ln_b_sb[:].rearrange("p (j d) -> p j d", j=4), ALU.add
                                 ).then_inc(ln_done, 1)

            def pool_means(half, j):
                window = POOLS[j]
                bufs, src = (probs_t, q_t), probs
                for m in range(j + 1):
                    lo, by, dst = 2 ** (m + 1) - 1, 2 ** m, bufs[m % 2]
                    settle(ve.tensor_tensor(dst[:, lo:HIST + HS], src[:, lo:HIST + HS],
                                            src[:, lo - by:HIST + HS - by], ALU.add))
                    src = dst
                last = ve.scalar_tensor_tensor(out=aux[:, HIST:HIST + HS], in0=src[:, HIST:HIST + HS],
                                               scalar=1.0 / window, in1=probs[:, HIST:HIST + HS],
                                               op0=ALU.mult, op1=ALU.subtract)
                if half == 0:
                    settle(last)
                    settle(ve.tensor_tensor(head_sum[:], src[:, HIST:2 * HIST], inv_sb[:, j, :], ALU.mult))
                    last = ve.tensor_tensor(aux[:, HIST:2 * HIST], head_sum[:], probs[:, HIST:2 * HIST],
                                            ALU.subtract)
                last.then_inc(pool_in, 1)

            def take_y(half, c):
                for st in range(ST):
                    n = 4 * half + c
                    if st == 0:
                        ve.wait_ge(group_done, GROUPS * half + G_OUT + 4 * c + 4)
                    ve.wait_ge(res_loaded[st], 16 * (n + 1))
                    ve.tensor_tensor(mix[:, 4 * st + c, :], N[st][:], residual[st][:, 0:512], ALU.add
                                     ).then_inc(y_evac, 1)

            def sum_ssq(half):
                ve.wait_ge(ssq_done, 16 * (half + 1))
                ve.tensor_reduce(ssq_sum[:], ssq[:], AX.X, ALU.add).then_inc(ssq_summed, 1)

            def norm_y(half, st):
                if st == 0:
                    ve.wait_ge(y_root, half + 1)
                    settle(ve.reciprocal(rstd_y[:], root_y[:]))
                row = mix[:, 4 * st:4 * st + 4, :].rearrange("p c d -> p (c d)")
                ve.scalar_tensor_tensor(out=row, in0=row, scalar=rstd_y[:, st:st + 1], in1=final_g_sb[:],
                                        op0=ALU.mult, op1=ALU.mult).then_inc(y_normed, 1)

            ve.wait_ge(norm_g_loaded, 16)
            for kt in range(4):
                x_lo(0, kt)
            split_lo(0)
            for kt in range(4, KT):
                x_lo(0, kt)
            ve.wait_ge(table_done, 1)
            ve.tensor_copy(table_sb[:], E[0][0:HEADS, 0:REL]).then_inc(table_copied, 1)
            ve.memset(k_t[:, :, 0:CHUNK], 0.0)
            ve.memset(v_prev[:], 0.0)
            settle(ve.memset(hist[:], 0.0))
            ve.wait_ge(consts_loaded, 16 * 11)
            settle(ve.memset(w_s_sb[64:128, :, 0:64], 0.0))

            for half in range(HALVES):
                for g in range(GROUPS):
                    G = GROUPS * half + g
                    if G + 1 < GROUPS * HALVES:
                        split_lo(G + 1)
                    if half == 1 and g == 0:
                        for kt in range(12, KT):
                            x_lo(1, kt)
                        take_y(0, 3)
                        sum_ssq(0)
                    if half == 1 and 1 <= g <= ST:
                        norm_y(0, g - 1)
                    if g == 1 and half == 1:
                        ve.tensor_copy(k_t[:, :, 0:CHUNK], k_t[:, :, HS:HS + CHUNK])
                    if g == 2:
                        ve.wait_ge(root_done, 2 * half + 2)
                        ve.reciprocal(rstd_row[:], rstd_row[:]).then_inc(rstd_done, 1)
                        ve.reciprocal(rstd_col[:], root_row[:]).then_inc(rstd_done, 1)
                        ve.wait_ge(rstd_done, 2 * half + 2)
                        for pair in range(2):
                            take(half, pair, k_t[:, pair, CHUNK:CHUNK + HS])
                        if half == 1:
                            ve.tensor_copy(v_prev[64:128, 0, :], v[64:128, ST - 1, :]).then_inc(v_saved, 1)
                        else:
                            ve.memset(v_prev[64:128, 0, :], 0.0).then_inc(v_saved, 1)
                    if g == G_VA:
                        ve.wait_ge(v_evac, ST * (half + 1))
                        ve.tensor_copy(v_prev[0:64, :, :], v[0:64, :, :]).then_inc(v_ready, 1)
                        ve.tensor_copy(v_prev[64:128, 1:ST, :], v[64:128, 0:ST - 1, :]).then_inc(v_ready, 1)
                    if g == G_Q:
                        for st in range(ST):
                            ve.wait_ge(va_evac, ST * half + st + 1)
                            for_stats = mix[:, M_A:M_A + 4, P * st:P * st + P]
                            settle(ve.bn_stats(bn[:, st, :], for_stats))
                            last = ve.bn_aggr(mean_var[:, st, :], bn[:, st, :])
                            if st < ST - 1:
                                settle(last)
                            else:
                                last.then_inc(ln_var, 1)
                    if g == G_Q + 1:
                        ve.wait_ge(ln_root, half + 1)
                        settle(ve.reciprocal(rstd_ln[:], root_ln[:]))
                    if g >= 1 and is_t(g - 1) and g > 2:
                        h = g - 1
                        ve.wait_ge(group_done, G)
                        if h < G_UA and h % 2 == 0:
                            m = PIECES * half + (h - G_Q)
                            if m >= 1:
                                ve.wait_ge(s_ready, m)
                            take(half, h, q_t[:, 0:HS])
                        elif G_C <= h and h % 2 == 0:
                            j = (h - G_C) // 2
                            settle(ve.tensor_copy(probs[:, 0:HIST], hist[:, j, :]))
                            take(half, h, probs[:, HIST:HIST + HS])
                            settle(ve.tensor_copy(hist[:, j, :], probs[:, HS:HS + HIST]))
                            if j == 0:
                                ve.wait_ge(o_ready, PIECES * (half + 1))
                            else:
                                ve.wait_ge(pool_ready, 4 * half + j)
                            pool_means(half, j)
                        else:
                            take(half, h, pre[:, 0:HS])
                    n = g - 1 - SLOT_S
                    if 0 <= n < PIECES:
                        softmax_scores(half, n)
                    n = g - 1 - SLOT_PV
                    if 0 <= n < PIECES:
                        m = PIECES * half + n
                        part = mix[:, n // 2, 256 * (n % 2):256 * (n % 2) + 256]
                        ve.wait_ge(o_ready, m + 1)
                        ve.tensor_tensor(part, O_bank[:, 0:256], part, ALU.mult).then_inc(o_evac, 1)
                    if G_Q + 1 <= g <= G_Q + ST:
                        layer_norm(g - G_Q - 1)
                    h = g - 1
                    if h >= 0 and is_gate(h):
                        gate_ready(half, h)
                        if h < G_UA:
                            settle(ve.tensor_scalar(act[:, 0:HS], act[:, 0:HS], 1.0, None, ALU.add))
                            settle(ve.reciprocal(act[:, 0:HS], act[:, 0:HS]))
                            if half == 1 and h == G_Q + 1:
                                ve.wait_ge(y_stored, 16 * ST)
                            ve.tensor_tensor(mix[:, (h - G_Q) // 2, :], pre[:, 0:HS], act[:, 0:HS], ALU.mult
                                             ).then_inc(gate_used, 1)
                            ve.wait_ge(gate_used, GATES * half + gate_index(h) + 1)
                        elif h < G_GA:
                            j = h - G_UA
                            ve.wait_ge(sgu_ready, 4 * half + j + 1)
                            settle(ve.tensor_tensor(
                                aux[:, 0:HS].rearrange("p (b i) -> p b i", b=4),
                                E[0][:].rearrange("p (b i) -> p b i", b=4),
                                b_s_sb[:, j, :].unsqueeze(1).broadcast_to([P, 4, P]), ALU.add))
                            ve.tensor_tensor(mix[:, M_A + j, :], aux[:, 0:HS], act[:, 0:HS], ALU.mult
                                             ).then_inc(gate_used, 1)
                            ve.wait_ge(gate_used, GATES * half + gate_index(h) + 1)
                        elif h < G_C:
                            j = h - G_GA
                            ve.tensor_tensor(mix[:, M_A + j, :], mix[:, M_A + j, :], act[:, 0:HS], ALU.mult
                                             ).then_inc(gate_used, 1)
                        else:
                            j = (h - G_C) // 2
                            ve.wait_ge(pool_ready, 4 * half + j + 1)
                            ve.scalar_tensor_tensor(out=mix[:, M_C + j, :], in0=E[1][:],
                                                    scalar=c_scale_sb[:, j:j + 1], in1=act[:, 0:HS],
                                                    op0=ALU.mult, op1=ALU.mult).then_inc(gate_used, 1)
                    n = g - 1 - SLOT_S
                    if 0 <= n < PIECES:
                        softmax_norm(half, n)
                    if g == G_OUT - 1:
                        for kt in range(KT - 1):
                            mix_lo(half, kt)
                    if g == G_OUT:
                        mix_lo(half, KT - 1)
                    if g >= G_OUT + 4 and g % 4 == 0:
                        take_y(half, (g - G_OUT) // 4 - 1)
                    if half == 0 and g > G_OUT + 12:
                        for kt in range(4 * (g - G_OUT - 13), 4 * (g - G_OUT - 12)):
                            x_lo(1, kt)
            take_y(1, 3)
            sum_ssq(1)
            for st in range(ST):
                norm_y(1, st)

        @block.tensor
        def _(pe):
            def w_tile(part, slot, at, n):
                return part[:, slot, at:at + n]

            def three(psum_out, stat, mov, first, last):
                pe.matmul(psum_out, stat[0], mov[0], start=first, stop=False)
                pe.matmul(psum_out, stat[0], mov[1], start=False, stop=False)
                return pe.matmul(psum_out, stat[1], mov[0], start=False, stop=last)

            def split_ready(G, s):
                pe.wait_ge(lo_done, 2 * G + s + 1)

            def t_tile(half, g):
                G, n = GROUPS * half + g, T_TILES * half + t_index(g)
                bank = T[t_index(g) % 2]
                if n >= 2:
                    pe.wait_ge(t_evac, n - 1)
                for kt in range(KT):
                    if kt % 8 == 0:
                        split_ready(G, kt // 8)
                    if g == 0:
                        pe.wait_ge(x_lo_done, KT * half + kt + 1)
                    at = P * kt
                    mm = three(bank[:], (w_tile(w_hi, G % 2, at, P), w_tile(w_lo, G % 2, at, P)),
                               (op_hi[:, kt, :], op_lo[:, kt, :]), kt == 0, kt == KT - 1)
                    if g == G_OUT - 1 and kt % 4 == 3 and kt < KT - 1:
                        mm.then_inc(x_read, 1)
                mm.then_inc(group_done, 1)

            def n_group(half, g, g0, width, kts):
                G = GROUPS * half + g
                for k, kt in enumerate(kts):
                    if k % (len(kts) // 2) == 0:
                        split_ready(G, k // (len(kts) // 2))
                    if g >= G_OUT and g < G_OUT + 4:
                        pe.wait_ge(m_lo_done, KT * half + kt + 1)
                    for st in range(ST):
                        pos = slice(P * st, P * st + P)
                        if kt == 0:
                            n_free(half, g, st)
                        mm = three(N[st][:, 0:width], (op_hi[:, kt, pos], op_lo[:, kt, pos]),
                                   (w_tile(w_hi, G % 2, width * k, width), w_tile(w_lo, G % 2, width * k, width)),
                                   kt == 0, kt == KT - 1)
                mm.then_inc(group_done, 1)

            def n_free(half, g, st):
                if g == G_V and half == 1:
                    pe.wait_ge(y_evac, ST * 3 + st + 1)
                if g == G_VA:
                    pe.wait_ge(v_evac, ST * half + st + 1)
                if g == G_OUT:
                    pe.wait_ge(o_evac, PIECES * (half + 1))
                if g > G_OUT:
                    pe.wait_ge(y_evac, ST * (4 * half + (g - G_OUT) // 4 - 1) + st + 1)

            def scores(half, n):
                i, tp, m = n // 2, n % 2, PIECES * half + n
                pair = i // 4
                pe.wait_ge(t_evac, T_TILES * half + t_index(G_Q + 2 * i) + 1)
                if n == 0:
                    pe.wait_ge(va_evac, ST * (half + 1))
                if m >= 1:
                    pe.wait_ge(shifted, 2 * m)
                for tl in range(2):
                    q0 = P * (2 * tp + tl)
                    k0, at = q0, P * tl
                    heads = [(S_bank[a], slice(64 * a, 64 * a + 64)) for a in range(2)]
                    for bank, h in heads:
                        pe.matmul(bank[:, at:at + 64], q_t[h, q0:q0 + P], k_t[h, pair, k0 + 64:k0 + 128],
                                  start=True, stop=True)
                    for bank, h in heads:
                        pe.matmul(bank[0:64, at + 64:at + 128], q_t[h, q0:q0 + 64],
                                  k_t[h, pair, k0:k0 + 64], start=True, stop=True)
                    for bank, h in heads:
                        mm = pe.matmul(bank[64:128, at + 64:at + 128], q_t[h, q0 + 64:q0 + 128],
                                       k_t[h, pair, k0 + 128:k0 + 192], start=True, stop=True)
                mm.then_inc(s_ready, 1)

            def transpose(half, n):
                m = PIECES * half + n
                pe.wait_ge(p_ready, m + 1)
                if m >= 1:
                    pe.wait_ge(pt_evac, m)
                for b in range(4):
                    mm = pe.transpose(PT_bank[:, P * b:P * b + P], probs[:, P * b:P * b + P], ident[:])
                mm.then_inc(pt_ready, 1)

            def values(half, n):
                i, tp, m = n // 2, n % 2, PIECES * half + n
                pe.wait_ge(pt_evac, m + 1)
                if m >= 1:
                    pe.wait_ge(o_evac, m)
                if n == 0:
                    pe.wait_ge(v_ready, 2 * (half + 1))
                for tl in range(2):
                    st = 2 * tp + tl
                    for a in range(2):
                        kv = 2 * (i // 4) + a
                        d, at = slice(64 * kv, 64 * kv + 64), (2 * a + tl) * P
                        for c, vals in enumerate((v_prev, v)):
                            mm = pe.matmul(O_bank[64 * a:64 * a + 64, P * tl + 64 * c:P * tl + 64 * c + 64],
                                           vals[:, st, d], probs_t[:, at + 64 * c:at + 64 * c + 64],
                                           start=True, stop=True)
                mm.then_inc(o_ready, 1)

            pe.wait_ge(consts_set, 3)
            pe.wait_ge(consts_loaded, 16 * 11)
            pe.matmul(E[0][0:HEADS, 0:REL], rel_sb[:], one_hot_sb[:], start=True, stop=True
                      ).then_inc(table_done, 1)
            for half in range(HALVES):
                for g in range(GROUPS):
                    if is_t(g):
                        t_tile(half, g)
                    elif g < G_VA:
                        n_group(half, g, G_V, 256, range(8 * (g - G_V), 8 * (g - G_V) + 8))
                    elif g < G_Q:
                        n_group(half, g, G_VA, 512, range(4 * (g - G_VA), 4 * (g - G_VA) + 4))
                    else:
                        k0 = 4 * ((g - G_OUT) % 4)
                        n_group(half, g, G_OUT, 512, range(k0, k0 + 4))
                    if g == 1:
                        pe.wait_ge(x_acc_done, (KT - 1) * (half + 1))
                        if half == 0:
                            pe.wait_ge(table_copied, 1)
                        pe.matmul(E[0][:], ones[:], rstd_row[:], start=True, stop=True)
                        for st in range(ST):
                            mm = pe.matmul(E[1][:, st:st + 1], rstd_row[:, P * st:P * st + P], ones[:, 0:1],
                                           start=True, stop=True)
                        mm.then_inc(stats_done, 1)
                    if 0 <= g - SLOT_PV < PIECES:
                        values(half, g - SLOT_PV)
                    if 0 <= g - SLOT_PT < PIECES:
                        transpose(half, g - SLOT_PT)
                    if 0 <= g - SLOT_S < PIECES:
                        scores(half, g - SLOT_S)
                    if G_UA <= g < G_GA:
                        j = g - G_UA
                        pe.wait_ge(ln_done, ST * (half + 1))
                        if j >= 1:
                            pe.wait_ge(gate_used, GATES * half + 8 + j)
                        for st in range(ST):
                            mm = pe.matmul(E[0][:, P * st:P * st + P], mix[:, M_A + j, P * st:P * st + P],
                                           w_s_sb[:, j, :], start=True, stop=True)
                        mm.then_inc(sgu_ready, 1)
                    if G_C <= g < G_OUT and g % 2 == 1:
                        j = (g - G_C) // 2
                        pe.wait_ge(pool_in, 4 * half + j + 1)
                        if j >= 1:
                            pe.wait_ge(gate_used, GATES * half + 16 + j)
                        pe.matmul(E[1][:], w_pool_sb[:, j, :], aux[:, HIST:HIST + HS], start=True, stop=True
                                  ).then_inc(pool_ready, 1)


def t5_bucket(rel):
    nb = REL_BUCKETS // 2
    exact = nb // 2
    n = np.abs(rel)
    large = exact + (np.log(np.maximum(n, 1).astype(np.float32) / exact)
                     / np.float32(math.log(REL_MAX_DIST / exact)) * (nb - exact)).astype(np.int32)
    return (rel > 0).astype(np.int32) * nb + np.where(n < exact, n, np.minimum(large, nb - 1))


def weight_stream(w_in, w_out):
    def tile(cols):
        return w_in[:, cols].reshape(KT, P, P).transpose(1, 0, 2).reshape(1, P, GW)

    def rows(m, at, width):
        part = m[:, at:at + width].reshape(KT, P, width).transpose(1, 0, 2)
        n = GW // width
        return part.reshape(P, KT // n, GW).transpose(1, 0, 2)

    span = lambda a, n: np.arange(a, a + n)
    pair = lambda base, i: np.concatenate([span(base + DH * h, DH) for h in tile_heads(i)])
    parts = [tile(span(2560 + P * p, P)) for p in range(2)]
    parts.append(rows(w_in, 2816, 256))
    parts.append(rows(w_in, 512, 512))
    for i in range(8):
        parts += [tile(pair(1536, i)), tile(pair(3072, i))]
    parts += [tile(span(P * j, P)) for j in range(4)]
    parts += [tile(span(1024 + P * j, P)) for j in range(4)]
    for j in range(4):
        parts += [tile(span(4096 + P * j, P)), tile(span(4608 + P * j, P))]
    order = np.concatenate([pair(512, i) for i in range(8)] + [span(0, 512), span(1536, 512)])
    mixed = w_out[order]
    parts += [rows(mixed, 512 * c, 512) for c in range(4)]
    return np.ascontiguousarray(np.concatenate(parts, axis=0))


def kernel(x, norm_g, w_in, a_ln_g, a_ln_b, a_w_s, a_b_s, b_sinks, rel_bias, c_w_pool, c_scale, w_out, final_g):
    import concourse.bacc as bacc
    from concourse.bass_utils import run_bass_kernel_spmd

    (x, norm_g, w_in, a_ln_g, a_ln_b, a_w_s, a_b_s, b_sinks, rel_bias, c_w_pool, c_scale, w_out, final_g) = (
        np.asarray(a) for a in (x, norm_g, w_in, a_ln_g, a_ln_b, a_w_s, a_b_s, b_sinks, rel_bias, c_w_pool,
                                c_scale, w_out, final_g))
    heads = np.array([h for i in range(8) for h in tile_heads(i)])
    one_hot = (t5_bucket(np.arange(REL) - 127)[None, :] == np.arange(REL_BUCKETS)[:, None]).astype(np.float32)
    counts = np.array([[1.0 / min(t + 1, window) for t in range(HIST)] for window in POOLS], np.float32)
    arrays = {
        "x": x[0],
        "x_t": x[0].T.reshape(4, 4, P, HALVES, HS).transpose(3, 0, 2, 1, 4).reshape(HALVES, 4, P, 4 * HS),
        "w": weight_stream(w_in[0], w_out[0]),
        "norm_g": norm_g[0].reshape(KT, P).T,
        "ln_g": a_ln_g, "ln_b": a_ln_b,
        "w_s": a_w_s[0].transpose(2, 0, 1).reshape(P, 4 * P),
        "b_s": a_b_s[0].reshape(1, 4 * P),
        "sinks": b_sinks[:, heads],
        "rel_bias": rel_bias[:, heads],
        "one_hot": one_hot,
        "inv_count": counts.reshape(1, 4 * HIST),
        "w_pool": c_w_pool[0].transpose(1, 0, 2).reshape(P, 4 * P),
        "c_scale": c_scale[0].reshape(4, P).T,
        "final_g": final_g.reshape(1, D),
    }
    arrays = {f"{k}_dram": np.ascontiguousarray(a) for k, a in arrays.items()}
    nc = bacc.Bacc("TRN2", target_bir_lowering=False, num_devices=1)
    args = [nc.dram_tensor(k, a.shape, mybir.dt.from_np(a.dtype), kind="ExternalInput").ap()
            for k, a in arrays.items()]
    out = nc.dram_tensor("out_dram", (SEQ, D), F32, kind="ExternalOutput").ap()
    build(nc, *args, out)
    r = run_bass_kernel_spmd(nc, [arrays], core_ids=[0])
    return r.results[0]["out_dram"].reshape(1, SEQ, D)
```

```python
import math
from contextlib import ExitStack

import numpy as np

import concourse.bass as bass
from concourse import mybir

ALU = mybir.AluOpType
ACT = mybir.ActivationFunctionType
AX = mybir.AxisListType
F32 = mybir.dt.float32
F32R = mybir.dt.float32r

P = 128
SEQ, D = 1024, 2048
HALVES = 2
HS = SEQ // HALVES
ST = HS // P
KT = D // P
CHUNK = 64
HEADS, KV_HEADS, DH = 16, 4, 64
EPS = 1e-6
REL_BUCKETS, REL_MAX_DIST = 32, 128
REL = 192
POOLS = (2, 4, 8, 16)
HIST = 16

G_K, G_V, G_VA, G_Q, G_UA, G_GA, G_C, G_OUT, GROUPS = 0, 2, 4, 8, 24, 28, 32, 40, 56
G_LAST = GROUPS - 4
TOTAL = 2 * GROUPS + 4
N_OUTPUTS = 6
G_LN = G_Q + 4
GW = 2048
PIECES = 16
SLOT_S, SLOT_PT, SLOT_PV = 9, 10, 11
GATES = 20
T_TILES = 34
M_A, M_C = 8, 12


def t_index(g):
    return g if g < G_V else g - G_Q + 2


def gate_index(g):
    if g < G_UA:
        return (g - G_Q) // 2
    if g < G_C:
        return 8 + g - G_UA
    return 16 + (g - G_C) // 2


def is_t(g):
    return g < G_V or G_Q <= g < G_OUT


def is_gate(g):
    return (G_Q <= g < G_UA and g % 2 == 1) or G_UA <= g < G_C or (G_C <= g < G_OUT and g % 2 == 1)


def split_index(G, sub):
    return 2 * sub + G if G < 2 else 2 * G + sub


def wait_loaded(eng, raw_loaded, first_loaded, G, sub):
    if G < 2:
        eng.wait_ge(first_loaded[2 * G + sub], 16)
    else:
        eng.wait_ge(raw_loaded[G % 2], 16 * (G // 2))


def wait_output(eng, bank_done, group_done, half, u, st):
    end = (G_VA, G_Q, G_OUT + 4, G_OUT + 8, G_OUT + 12, GROUPS)[u]
    if half == 1 and u == N_OUTPUTS - 1:
        last, end = (1, end) if st < 2 else (3, end + 4)
    else:
        last = ST - 1
    if st == last:
        eng.wait_ge(group_done, GROUPS * half + end)
    else:
        eng.wait_ge(bank_done[st], N_OUTPUTS * half + u + 1)


def tile_heads(i):
    return 8 * (i // 4) + i % 4, 8 * (i // 4) + 4 + i % 4


def build(nc, x, x_t, w, norm_g, ln_g, ln_b, w_s, b_s, sinks, rel_bias, one_hot, inv_count, w_pool,
          c_scale, final_g, out):
    table = nc.dram_tensor("rel_table", [CHUNK, HEADS, REL], F32).ap()
    with ExitStack() as ctx:
        def sb(name, shape, dt=F32):
            return ctx.enter_context(nc.sbuf_tensor(name, shape, dt))

        def psum(name):
            return ctx.enter_context(nc.psum_tensor(name, [P, 512], F32))

        def sem(name):
            return ctx.enter_context(nc.semaphore(name))

        op_hi = sb("op_hi", [P, KT, HS], F32R)
        op_lo = sb("op_lo", [P, KT, HS], F32R)
        mix = sb("mix", [P, KT, HS])
        raw = sb("raw", [P, 2, GW])
        w_hi = sb("w_hi", [P, 2, GW], F32R)
        w_lo = sb("w_lo", [P, 2, GW], F32R)
        x_raw = sb("x_raw", [P, 2, HS])
        x_sq = sb("x_sq", [P, 2, HS])
        rstd_row = sb("rstd_row", [P, HS])
        k_t = sb("k_t", [P, 2, CHUNK + HS])
        v = sb("v", [P, ST, KV_HEADS * DH])
        v_prev = sb("v_prev", [P, ST, KV_HEADS * DH])
        probs = sb("probs", [P, 528])
        probs_t = sb("probs_t", [P, 528])
        q_t = sb("q_t", [P, 528])
        pre = sb("pre", [P, 528])
        act = sb("act", [P, 528])
        aux = sb("aux", [P, 528])
        norm_g_sb = sb("norm_g_sb", [P, KT])
        ln_g_sb = sb("ln_g_sb", [P, 512])
        ln_b_sb = sb("ln_b_sb", [P, 512])
        w_s_sb = sb("w_s_sb", [P, 4, P])
        b_s_sb = sb("b_s_sb", [P, 4, P])
        sink_sb = sb("sink_sb", [P, HEADS])
        rel_sb = sb("rel_sb", [REL_BUCKETS, HEADS])
        one_hot_sb = sb("one_hot_sb", [REL_BUCKETS, REL])
        table_sb = sb("table_sb", [HEADS, REL])
        bias = sb("bias", [P, HEADS, P])
        inv_sb = sb("inv_sb", [P, 4, HIST])
        w_pool_sb = sb("w_pool_sb", [P, 4, P])
        c_scale_sb = sb("c_scale_sb", [P, 4])
        final_g_sb = sb("final_g_sb", [P, D])
        ones = sb("ones", [P, P])
        ident = sb("ident", [P, P])
        hist = sb("hist", [P, 4, HIST])
        head_sum = sb("head_sum", [P, HIST])
        eps_sb = sb("eps_sb", [P, 1])
        root_row = sb("root_row", [P, 4])
        rstd_col = sb("rstd_col", [P, 4])
        root_ln = sb("root_ln", [P, 4])
        rstd_ln = sb("rstd_ln", [P, 4])
        bn = sb("bn", [P, 4, 6])
        mean_var = sb("mean_var", [P, 4, 2])
        row_max = sb("row_max", [P, 4])
        sink_d = sb("sink_d", [P, 4])
        sink_e = sb("sink_e", [P, 4])
        row_sum = sb("row_sum", [P, 4])
        row_inv = sb("row_inv", [P, 4])
        ssq = sb("ssq", [P, ST, 4])
        ssq_sum = sb("ssq_sum", [P, ST])
        root_y = sb("root_y", [P, ST])
        rstd_y = sb("rstd_y", [P, ST])
        residual = [probs, probs_t, q_t, aux]

        T = [psum(f"t_bank{i}") for i in range(2)]
        N = [psum(f"n_bank{i}") for i in range(4)]
        E = [psum(f"e_bank{i}") for i in range(2)]
        S_bank, PT_bank, O_bank = (N[0], N[3]), N[1], N[2]

        raw_loaded = [sem(f"raw_loaded{i}") for i in range(2)]
        first_loaded = [sem(f"first_loaded{i}") for i in range(4)]
        hi_done, lo_done, group_done = sem("hi_done"), sem("lo_done"), sem("group_done")
        norm_g_loaded = sem("norm_g_loaded")
        x_loaded = [sem(f"x_loaded{i}") for i in range(KT // 2)]
        x_raw_loaded = [sem(f"x_raw_loaded{i}") for i in range(2)]
        bank_done = [sem(f"bank_done{i}") for i in range(ST)]
        x_hi_done, x_lo_done, x_sq_done, x_acc_done = (sem("x_hi_done"), sem("x_lo_done"), sem("x_sq_done"),
                                                       sem("x_acc_done"))
        x_read = sem("x_read")
        m_hi_done, m_lo_done = sem("m_hi_done"), sem("m_lo_done")
        consts_loaded, consts_set = sem("consts_loaded"), sem("consts_set")
        table_done, table_copied, table_stored, bias_loaded = (sem("table_done"), sem("table_copied"),
                                                               sem("table_stored"), sem("bias_loaded"))
        stats_done, root_done, rstd_done = sem("stats_done"), sem("root_done"), sem("rstd_done")
        t_evac, v_evac, v_saved, va_evac = sem("t_evac"), sem("v_evac"), sem("v_saved"), sem("va_evac")
        v_ready = sem("v_ready")
        ln_var, ln_root, ln_done = sem("ln_var"), sem("ln_root"), sem("ln_done")
        s_ready, shifted, exp_done, p_ready = sem("s_ready"), sem("shifted"), sem("exp_done"), sem("p_ready")
        pt_ready, pt_evac, o_ready, o_evac = sem("pt_ready"), sem("pt_evac"), sem("o_ready"), sem("o_evac")
        gate_fn, gate_used = sem("gate_fn"), sem("gate_used")
        sgu_ready, pool_in, pool_ready = sem("sgu_ready"), sem("pool_in"), sem("pool_ready")
        res_loaded = [sem(f"res_loaded{i}") for i in range(ST)]
        y_evac, y_scaled, y_inverted, ssq_done, ssq_summed, y_root, y_normed, y_stored = (sem("y_evac"), sem("y_scaled"), sem("y_inverted"), sem("ssq_done"), sem("ssq_summed"), sem("y_root"),
                                                        sem("y_normed"), sem("y_stored"))
        dve_settled, act_settled, pool_settled = sem("dve_settled"), sem("act_settled"), sem("pool_settled")

        block = ctx.enter_context(nc.Block())

        @block.sync
        def _(sp):
            def store(sp, half, st):
                if half == 0:
                    sp.wait_ge(y_normed, st + 1)
                else:
                    sp.wait_ge(y_normed, ST + 2 * st + 2)
                    sp.wait_ge(y_scaled, st + 1)
                s0 = HS * half + P * st
                sp.dma_start(out[s0:s0 + P, :], mix[:, 4 * st:4 * st + 4, :].rearrange("p c d -> p (c d)")
                             ).then_inc(y_stored, 16)

            def load_group(G):
                sp.wait_ge(lo_done, max(2 * (G - 1), 4))
                g = G % GROUPS if G < 2 * GROUPS else G % GROUPS + G_LAST
                sp.dma_start(raw[:, G % 2, :], w[g]).then_inc(raw_loaded[G % 2], 16)

            def load_first(G, sub):
                sp.dma_start(raw[:, G, 1024 * sub:1024 * sub + 1024], w[G, :, 1024 * sub:1024 * sub + 1024]
                             ).then_inc(first_loaded[2 * G + sub], 16)

            def load_x(a):
                sp.dma_start(mix[:, 2 * a:2 * a + 2, :].rearrange("p k s -> p (k s)"),
                             x_t[0, a // 2, :, 1024 * (a % 2):1024 * (a % 2) + 1024]).then_inc(x_loaded[a], 16)

            sp.dma_start(norm_g_sb[:], norm_g).then_inc(norm_g_loaded, 16)
            load_first(0, 0)
            for a in range(KT // 4):
                load_x(a)
            load_first(1, 0)
            for a in range(KT // 4, KT // 2):
                load_x(a)
            load_first(0, 1)
            load_first(1, 1)

            def rows(a, n):
                return bass.AP(a.tensor, 0, [[0, P], [1, n]])

            for dst, src in ((rel_sb[:], rel_bias), (one_hot_sb[:], one_hot), (sink_sb[:], rows(sinks, HEADS)),
                             (ln_g_sb[:], rows(ln_g, 512)), (ln_b_sb[:], rows(ln_b, 512)),
                             (w_s_sb[:].rearrange("p g i -> p (g i)"), w_s),
                             (b_s_sb[:].rearrange("p g i -> p (g i)"), rows(b_s, 512)),
                             (inv_sb[:].rearrange("p g i -> p (g i)"), rows(inv_count, 4 * HIST)),
                             (w_pool_sb[:].rearrange("p g i -> p (g i)"), w_pool), (c_scale_sb[:], c_scale),
                             (final_g_sb[:], rows(final_g, D))):
                sp.dma_start(dst, src).then_inc(consts_loaded, 16)

            for half in range(HALVES):
                for g in range(GROUPS + 4 * half):
                    G = GROUPS * half + g
                    if G + 2 < TOTAL:
                        load_group(G + 2)
                    if half == 0 and g == 2:
                        sp.wait_ge(table_copied, 1)
                        sp.dma_start(table.rearrange("q h r -> h q r"),
                                     table_sb[:].unsqueeze(1).broadcast_to([HEADS, CHUNK, REL])).then_inc(table_stored, 16)
                        sp.wait_ge(table_stored, 16)
                        for q0, q1, s0, s1, at in ((0, 64, 0, 64, 127), (0, 64, 64, 128, 63), (64, 128, 0, 128, 63)):
                            sp.dma_start(bias[q0:q1, :, s0:s1],
                                         bass.AP(table.tensor, at, [[HEADS * REL - 1, CHUNK], [REL, HEADS], [1, s1 - s0]])
                                         ).then_inc(bias_loaded, 16)
                    if G_OUT <= g < GROUPS and g % 4 == 1:
                        c = (g - G_OUT) // 4
                        n = 4 * half + c
                        if c == 0:
                            sp.wait_ge(m_lo_done, KT * (half + 1))
                        else:
                            sp.wait_ge(y_evac, ST * n)
                        for st in range(ST):
                            s0 = HS * half + P * st
                            sp.dma_start(residual[st][:, 0:512], x[s0:s0 + P, 512 * c:512 * c + 512]
                                         ).then_inc(res_loaded[st], 16)
                    if half == 0 and g >= G_LAST:
                        for kt in range(4 * (g - G_LAST), 4 * (g - G_LAST) + 4):
                            if kt >= 2:
                                sp.wait_ge(x_lo_done, KT + kt - 1)
                                sp.wait_ge(x_sq_done, KT + kt - 1)
                            sp.dma_start(x_raw[:, kt % 2, :], x_t[1, kt // 4, :, HS * (kt % 4):HS * (kt % 4) + HS]
                                         ).then_inc(x_raw_loaded[kt % 2], 16)
                    if half == 1 and 1 <= g <= ST:
                        store(sp, 0, g - 1)
                    if half == 1 and g == GROUPS + 1:
                        for st in range(2):
                            store(sp, 1, st)
            for st in range(2, ST):
                store(sp, 1, st)
            sp.wait_ge(y_stored, 16 * ST * HALVES)

        @block.gpsimd
        def _(pool):
            settled = [0]

            def settle(ins):
                settled[0] += 1
                ins.then_inc(pool_settled, 1)
                pool.wait_ge(pool_settled, settled[0])

            pool.memset(ones[:], 1.0).then_inc(consts_set, 1)
            pool.memset(eps_sb[:], EPS).then_inc(consts_set, 1)
            settle(pool.memset(ident[:], 0.0))
            pool.affine_select(out=ident[:], in_=ident[:], compare_op=ALU.not_equal, fill=1.0, base=0,
                               pattern=[[-1, P]], channel_multiplier=1).then_inc(consts_set, 1)

            for half in range(HALVES):
                for kt in range(1, KT):
                    pool.wait_ge(x_sq_done, KT * half + kt + 1)
                    pool.tensor_tensor(rstd_row[:], rstd_row[:], x_sq[:, kt % 2, :], ALU.add
                                       ).then_inc(x_acc_done, 1)
                    pool.wait_ge(x_acc_done, (KT - 1) * half + kt)

        @block.scalar
        def _(sc):
            def square_y(half, c, sts=range(ST)):
                for st in sts:
                    n = ST * (4 * half + c) + st
                    sc.wait_ge(y_evac, n + 1)
                    if n >= 1:
                        sc.wait_ge(ssq_done, n)
                    sc.activation(act[:, 0:512], mix[:, 4 * st + c, :], ACT.Square,
                                  accum_out=ssq[:, st, c:c + 1]).then_inc(ssq_done, 1)

            def root_of_y(half):
                sc.wait_ge(ssq_summed, half + 1)
                sc.activation(root_y[:], ssq_sum[:], ACT.Sqrt, bias=eps_sb[:], scale=1.0 / D
                              ).then_inc(y_root, 1)

            def finish_pair(p):
                two = slice(2 * p, 2 * p + 2)
                sc.wait_ge(ssq_summed, 2 + p)
                sc.activation(root_y[:, two], ssq_sum[:, two], ACT.Sqrt, bias=eps_sb[:], scale=1.0 / D
                              ).then_inc(y_root, 1)
                sc.wait_ge(y_inverted, 2 + p)
                for st in range(2 * p, 2 * p + 2):
                    row = mix[:, 4 * st:4 * st + 2, :].rearrange("p c d -> p (c d)")
                    sc.activation(row, row, ACT.Copy, scale=rstd_y[:, st:st + 1]).then_inc(y_scaled, 1)

            def split_hi(G, subs=(0, 1)):
                for sub in subs:
                    wait_loaded(sc, raw_loaded, first_loaded, G, sub)
                    if G >= 2:
                        sc.wait_ge(group_done, G - 1)
                    part = slice(1024 * sub, 1024 * sub + 1024)
                    sc.activation(w_hi[:, G % 2, part], raw[:, G % 2, part], ACT.Copy).then_inc(hi_done, 1)

            def x_hi(half, kt):
                src = mix[:, kt, :] if half == 0 else x_raw[:, kt % 2, :]
                if half == 0:
                    sc.wait_ge(x_loaded[kt // 2], 16)
                else:
                    sc.wait_ge(x_raw_loaded[kt % 2], 16 * (kt // 2 + 1))
                    sc.wait_ge(group_done, G_LAST + kt // 4 + 1)
                sc.activation(op_hi[:, kt, :], src, ACT.Copy, scale=norm_g_sb[:, kt:kt + 1]
                              ).then_inc(x_hi_done, 1)
                if kt == 0:
                    if half == 1:
                        sc.wait_ge(t_evac, T_TILES)
                    sc.activation(rstd_row[:], src, ACT.Square).then_inc(x_sq_done, 1)
                else:
                    if kt >= 3:
                        sc.wait_ge(x_acc_done, (KT - 1) * half + kt - 2)
                    sc.activation(x_sq[:, kt % 2, :], src, ACT.Square).then_inc(x_sq_done, 1)

            def mix_hi(half, kt):
                if kt < 12:
                    sc.wait_ge(x_read, 3 * half + kt // 4 + 1)
                else:
                    sc.wait_ge(group_done, GROUPS * half + G_OUT)
                sc.wait_ge(gate_used, GATES * (half + 1) - (1 if kt < KT - 1 else 0))
                sc.activation(op_hi[:, kt, :], mix[:, kt, :], ACT.Copy).then_inc(m_hi_done, 1)

            sc.wait_ge(norm_g_loaded, 16)
            for G, sub, kts in ((0, 0, range(8)), (1, 0, range(8, KT)), (0, 1, ()), (1, 1, ())):
                split_hi(G, (sub,))
                for kt in kts:
                    x_hi(0, kt)
            sc.wait_ge(consts_set, 3)
            for half in range(HALVES):
                for g in range(GROUPS + 4 * half):
                    G = GROUPS * half + g
                    if g == G_VA:
                        sc.wait_ge(v_saved, half + 1)
                        for st in range(ST):
                            wait_output(sc, bank_done, group_done, half, 0, st)
                            sc.activation(v[:, st, :], N[st][:, 0:256], ACT.Copy, scale=rstd_col[:, st:st + 1]
                                          ).then_inc(v_evac, 1)
                    if g == G_Q:
                        if half == 1:
                            sc.wait_ge(y_stored, 16 * ST)
                        for st in range(ST):
                            wait_output(sc, bank_done, group_done, half, 1, st)
                            sc.activation(mix[:, M_A:M_A + 4, P * st:P * st + P],
                                          N[st][:].rearrange("p (j d) -> p j d", j=4), ACT.Gelu,
                                          scale=rstd_col[:, st:st + 1]).then_inc(va_evac, 1)
                    if 2 <= G + 1 < TOTAL:
                        split_hi(G + 1)
                    if half == 1 and g == 0:
                        for kt in range(12, KT):
                            x_hi(1, kt)
                    if g == G_V + 1:
                        sc.wait_ge(stats_done, half + 1)
                        sc.activation(rstd_row[:], E[0][:], ACT.Sqrt, bias=eps_sb[:], scale=1.0 / D
                                      ).then_inc(root_done, 1)
                        sc.activation(root_row[:], E[1][:, 0:4], ACT.Sqrt, bias=eps_sb[:], scale=1.0 / D
                                      ).then_inc(root_done, 1)
                    if g == G_LN - 1:
                        sc.wait_ge(ln_var, half + 1)
                        sc.activation(root_ln[:], mean_var[:, :, 1], ACT.Sqrt, bias=eps_sb[:]
                                      ).then_inc(ln_root, 1)
                    if g >= 1 and is_gate(g - 1):
                        n = GATES * half + gate_index(g - 1)
                        sc.wait_ge(t_evac, T_TILES * half + t_index(g - 1) + 1)
                        if n >= 1:
                            sc.wait_ge(gate_used, n)
                        if g - 1 < G_UA:
                            sc.activation(act[:, 0:HS], pre[:, 0:HS], ACT.Tanh, scale=0.5).then_inc(gate_fn, 1)
                        else:
                            sc.activation(act[:, 0:HS], pre[:, 0:HS], ACT.Gelu if g - 1 < G_GA else ACT.Silu
                                          ).then_inc(gate_fn, 1)
                    n = g - 1 - SLOT_PT
                    if 0 <= n < PIECES:
                        m = PIECES * half + n
                        sc.wait_ge(pt_ready, m + 1)
                        if m >= 1:
                            sc.wait_ge(o_ready, m)
                        sc.activation(probs_t[:, 0:512], PT_bank[:], ACT.Copy).then_inc(pt_evac, 1)
                    n = g - 1 - SLOT_S
                    if 0 <= n < PIECES:
                        m = PIECES * half + n
                        sc.wait_ge(shifted, 2 * m + 2)
                        sc.activation(sink_e[:], sink_d[:], ACT.Exp).then_inc(exp_done, 1)
                        sc.activation(probs[:, 0:512], probs[:, 0:512], ACT.Exp).then_inc(exp_done, 1)
                    if g == G_OUT - 1:
                        for kt in range(KT - 1):
                            mix_hi(half, kt)
                    if g == G_OUT:
                        mix_hi(half, KT - 1)
                    if G_OUT + 4 <= g < GROUPS and g % 4 == 0:
                        square_y(half, (g - G_OUT) // 4 - 1)
                    if half == 1 and g == 0:
                        square_y(0, 3)
                        root_of_y(0)
                    if half == 1 and g == GROUPS:
                        square_y(1, 3, range(2))
                        finish_pair(0)
                    if half == 0 and g > G_LAST:
                        for kt in range(4 * (g - G_LAST - 1), 4 * (g - G_LAST)):
                            x_hi(1, kt)
            square_y(1, 3, range(2, ST))
            finish_pair(1)

        @block.vector
        def _(ve):
            settled = [0]

            def settle(ins):
                settled[0] += 1
                ins.then_inc(dve_settled, 1)
                ve.wait_ge(dve_settled, settled[0])

            def split_lo(G, subs=(0, 1)):
                for sub in subs:
                    ve.wait_ge(hi_done, split_index(G, sub) + 1)
                    part = slice(1024 * sub, 1024 * sub + 1024)
                    ve.tensor_tensor(w_lo[:, G % 2, part], raw[:, G % 2, part], w_hi[:, G % 2, part].bitcast(F32),
                                     ALU.subtract).then_inc(lo_done, 1)

            def x_lo(half, kt):
                src = mix[:, kt, :] if half == 0 else x_raw[:, kt % 2, :]
                ve.wait_ge(x_hi_done, KT * half + kt + 1)
                ve.scalar_tensor_tensor(out=op_lo[:, kt, :], in0=src, scalar=norm_g_sb[:, kt:kt + 1],
                                        in1=op_hi[:, kt, :].bitcast(F32), op0=ALU.mult, op1=ALU.subtract
                                        ).then_inc(x_lo_done, 1)

            def mix_lo(half, kt):
                ve.wait_ge(m_hi_done, KT * half + kt + 1)
                ve.tensor_tensor(op_lo[:, kt, :], mix[:, kt, :], op_hi[:, kt, :].bitcast(F32), ALU.subtract
                                 ).then_inc(m_lo_done, 1)

            def take(half, g, dst):
                ve.tensor_tensor(dst, T[t_index(g) % 2][:], rstd_row[:], ALU.mult).then_inc(t_evac, 1)
                ve.wait_ge(t_evac, T_TILES * half + t_index(g) + 1)

            def gate_ready(half, g):
                ve.wait_ge(gate_fn, GATES * half + gate_index(g) + 1)

            def softmax_scores(half, n):
                i, tp, m = n // 2, n % 2, PIECES * half + n
                ve.wait_ge(s_ready, m + 1)
                if m == 0:
                    ve.wait_ge(bias_loaded, 48)
                for a in range(2):
                    settle(ve.scalar_tensor_tensor(
                        out=probs[:, 256 * a:256 * a + 256].rearrange("p (t s) -> p t s", t=2),
                        in0=S_bank[a][:, 0:256].rearrange("p (t s) -> p t s", t=2), scalar=DH ** -0.5,
                        in1=bias[:, 2 * i + a, :].unsqueeze(1).broadcast_to([P, 2, P]),
                        op0=ALU.mult, op1=ALU.add))
                if half == 0 and tp == 0:
                    off = probs[0:64, 0:512].rearrange("p (h t s) -> p h t s", h=2, t=2)[:, :, 0, 64:128]
                    settle(ve.memset(off, -1e30))
                scores = probs[:, 0:512].rearrange("p (b s) -> p b s", b=4)
                sink4 = sink_sb[:, 2 * i:2 * i + 2].unsqueeze(2).broadcast_to([P, 2, 2])
                settle(ve.tensor_reduce(row_max[:], scores, AX.X, ALU.max))
                settle(ve.tensor_tensor(row_max[:].rearrange("p (h t) -> p h t", h=2),
                                        row_max[:].rearrange("p (h t) -> p h t", h=2), sink4, ALU.max))
                ve.tensor_tensor(sink_d[:].rearrange("p (h t) -> p h t", h=2), sink4,
                                 row_max[:].rearrange("p (h t) -> p h t", h=2), ALU.subtract
                                 ).then_inc(shifted, 1)
                ve.tensor_tensor(scores, scores, row_max[:].unsqueeze(2).broadcast_to([P, 4, P]),
                                 ALU.subtract).then_inc(shifted, 1)

            def softmax_norm(half, n):
                m = PIECES * half + n
                ve.wait_ge(exp_done, 2 * m + 2)
                scores = probs[:, 0:512].rearrange("p (b s) -> p b s", b=4)
                settle(ve.tensor_reduce(row_sum[:], scores, AX.X, ALU.add))
                settle(ve.tensor_tensor(row_sum[:], row_sum[:], sink_e[:], ALU.add))
                settle(ve.reciprocal(row_inv[:], row_sum[:]))
                ve.tensor_tensor(scores, scores, row_inv[:].unsqueeze(2).broadcast_to([P, 4, P]),
                                 ALU.mult).then_inc(p_ready, 1)

            def layer_norm(st):
                view = mix[:, M_A:M_A + 4, P * st:P * st + P]
                settle(ve.tensor_scalar(view, view, mean_var[:, st, 0:1], rstd_ln[:, st:st + 1],
                                        ALU.subtract, ALU.mult))
                settle(ve.tensor_tensor(view, view, ln_g_sb[:].rearrange("p (j d) -> p j d", j=4), ALU.mult))
                ve.tensor_tensor(view, view, ln_b_sb[:].rearrange("p (j d) -> p j d", j=4), ALU.add
                                 ).then_inc(ln_done, 1)

            def pool_means(half, j):
                window = POOLS[j]
                bufs, src = (probs_t, q_t), probs
                for m in range(j + 1):
                    lo, by, dst = 2 ** (m + 1) - 1, 2 ** m, bufs[m % 2]
                    settle(ve.tensor_tensor(dst[:, lo:HIST + HS], src[:, lo:HIST + HS],
                                            src[:, lo - by:HIST + HS - by], ALU.add))
                    src = dst
                last = ve.scalar_tensor_tensor(out=aux[:, HIST:HIST + HS], in0=src[:, HIST:HIST + HS],
                                               scalar=1.0 / window, in1=probs[:, HIST:HIST + HS],
                                               op0=ALU.mult, op1=ALU.subtract)
                if half == 0:
                    settle(last)
                    settle(ve.tensor_tensor(head_sum[:], src[:, HIST:2 * HIST], inv_sb[:, j, :], ALU.mult))
                    last = ve.tensor_tensor(aux[:, HIST:2 * HIST], head_sum[:], probs[:, HIST:2 * HIST],
                                            ALU.subtract)
                last.then_inc(pool_in, 1)

            def take_y(half, c, sts=range(ST)):
                for st in sts:
                    wait_output(ve, bank_done, group_done, half, 2 + c, st)
                    ve.wait_ge(res_loaded[st], 16 * (4 * half + c + 1))
                    ve.tensor_tensor(mix[:, 4 * st + c, :], N[st][:], residual[st][:, 0:512], ALU.add
                                     ).then_inc(y_evac, 1)

            def sum_ssq():
                ve.wait_ge(ssq_done, 16)
                ve.tensor_reduce(ssq_sum[:], ssq[:], AX.X, ALU.add).then_inc(ssq_summed, 1)

            def norm_y(st):
                if st == 0:
                    ve.wait_ge(y_root, 1)
                    ve.reciprocal(rstd_y[:], root_y[:]).then_inc(y_inverted, 1)
                    ve.wait_ge(y_inverted, 1)
                row = mix[:, 4 * st:4 * st + 4, :].rearrange("p c d -> p (c d)")
                ve.scalar_tensor_tensor(out=row, in0=row, scalar=rstd_y[:, st:st + 1], in1=final_g_sb[:],
                                        op0=ALU.mult, op1=ALU.mult).then_inc(y_normed, 1)

            def weigh_y(c):
                ve.wait_ge(ssq_done, 16 + 4 * c + 4)
                for st in range(ST):
                    tile = mix[:, 4 * st + c, :]
                    settle(ve.tensor_tensor(tile, tile, final_g_sb[:, 512 * c:512 * c + 512], ALU.mult))

            def finish_pair(p):
                two = slice(2 * p, 2 * p + 2)
                take_y(1, 3, range(2 * p, 2 * p + 2))
                ve.wait_ge(ssq_done, 30 + 2 * p)
                ve.tensor_reduce(ssq_sum[:, two], ssq[:, two, :], AX.X, ALU.add).then_inc(ssq_summed, 1)
                ve.wait_ge(y_root, 2 + p)
                ve.reciprocal(rstd_y[:, two], root_y[:, two]).then_inc(y_inverted, 1)
                ve.wait_ge(y_inverted, 2 + p)
                for st in range(2 * p, 2 * p + 2):
                    tile = mix[:, 4 * st + 2, :]
                    ve.tensor_scalar(tile, tile, rstd_y[:, st:st + 1], None, ALU.mult).then_inc(y_normed, 1)
                    tile = mix[:, 4 * st + 3, :]
                    ve.scalar_tensor_tensor(out=tile, in0=tile, scalar=rstd_y[:, st:st + 1],
                                            in1=final_g_sb[:, 1536:2048], op0=ALU.mult, op1=ALU.mult
                                            ).then_inc(y_normed, 1)

            ve.wait_ge(norm_g_loaded, 16)
            for G, sub, kts in ((0, 0, range(8)), (1, 0, range(8, KT)), (0, 1, ()), (1, 1, ())):
                split_lo(G, (sub,))
                for kt in kts:
                    x_lo(0, kt)
            ve.memset(k_t[:, :, 0:CHUNK], 0.0)
            ve.memset(v_prev[:], 0.0)
            settle(ve.memset(hist[:], 0.0))
            ve.wait_ge(consts_loaded, 16 * 11)
            settle(ve.memset(w_s_sb[64:128, :, 0:64], 0.0))

            for half in range(HALVES):
                for g in range(GROUPS + 4 * half):
                    G = GROUPS * half + g
                    if G_OUT + 4 <= g < GROUPS and g % 4 == 0:
                        take_y(half, (g - G_OUT) // 4 - 1)
                    if half == 1 and g == 0:
                        take_y(0, 3)
                    if half == 1 and g == GROUPS:
                        finish_pair(0)
                    if 2 <= G + 1 < TOTAL:
                        split_lo(G + 1)
                    if half == 1 and g == 0:
                        for kt in range(12, KT):
                            x_lo(1, kt)
                        sum_ssq()
                    if half == 1 and 1 <= g <= ST:
                        norm_y(g - 1)
                    if half == 1 and g in (G_OUT + 6, G_OUT + 10, G_OUT + 14):
                        weigh_y((g - G_OUT - 6) // 4)
                    if g == 1 and half == 0:
                        ve.wait_ge(table_done, 1)
                        ve.tensor_copy(table_sb[:], E[0][0:HEADS, 0:REL]).then_inc(table_copied, 1)
                    if g == 1 and half == 1:
                        ve.tensor_copy(k_t[:, :, 0:CHUNK], k_t[:, :, HS:HS + CHUNK])
                    if g == G_V + 1:
                        ve.wait_ge(root_done, 2 * half + 2)
                        ve.reciprocal(rstd_row[:], rstd_row[:]).then_inc(rstd_done, 1)
                        ve.reciprocal(rstd_col[:], root_row[:]).then_inc(rstd_done, 1)
                        ve.wait_ge(rstd_done, 2 * half + 2)
                        for pair in range(2):
                            take(half, pair, k_t[:, pair, CHUNK:CHUNK + HS])
                        if half == 1:
                            ve.tensor_copy(v_prev[64:128, 0, :], v[64:128, ST - 1, :]).then_inc(v_saved, 1)
                        else:
                            ve.memset(v_prev[64:128, 0, :], 0.0).then_inc(v_saved, 1)
                    if g == G_VA:
                        ve.wait_ge(v_evac, ST * (half + 1))
                        ve.tensor_copy(v_prev[0:64, :, :], v[0:64, :, :]).then_inc(v_ready, 1)
                        ve.tensor_copy(v_prev[64:128, 1:ST, :], v[64:128, 0:ST - 1, :]).then_inc(v_ready, 1)
                    if g == G_Q:
                        for st in range(ST):
                            ve.wait_ge(va_evac, ST * half + st + 1)
                            for_stats = mix[:, M_A:M_A + 4, P * st:P * st + P]
                            settle(ve.bn_stats(bn[:, st, :], for_stats))
                            last = ve.bn_aggr(mean_var[:, st, :], bn[:, st, :])
                            if st < ST - 1:
                                settle(last)
                            else:
                                last.then_inc(ln_var, 1)
                    if g == G_LN:
                        ve.wait_ge(ln_root, half + 1)
                        settle(ve.reciprocal(rstd_ln[:], root_ln[:]))
                    if g > G_Q and is_t(g - 1):
                        h = g - 1
                        ve.wait_ge(group_done, G)
                        if h < G_UA and h % 2 == 0:
                            m = PIECES * half + (h - G_Q)
                            if m >= 1:
                                ve.wait_ge(s_ready, m)
                            take(half, h, q_t[:, 0:HS])
                        elif G_C <= h and h % 2 == 0:
                            j = (h - G_C) // 2
                            settle(ve.tensor_copy(probs[:, 0:HIST], hist[:, j, :]))
                            take(half, h, probs[:, HIST:HIST + HS])
                            settle(ve.tensor_copy(hist[:, j, :], probs[:, HS:HS + HIST]))
                            if j == 0:
                                ve.wait_ge(o_ready, PIECES * (half + 1))
                            else:
                                ve.wait_ge(pool_ready, 4 * half + j)
                            pool_means(half, j)
                        else:
                            take(half, h, pre[:, 0:HS])
                    n = g - 1 - SLOT_S
                    if 0 <= n < PIECES:
                        softmax_scores(half, n)
                    n = g - 1 - SLOT_PV
                    if 0 <= n < PIECES:
                        m = PIECES * half + n
                        part = mix[:, n // 2, 256 * (n % 2):256 * (n % 2) + 256]
                        ve.wait_ge(o_ready, m + 1)
                        ve.scalar_tensor_tensor(out=part, in0=O_bank[:, 0:256], scalar=0.5, in1=part,
                                                op0=ALU.mult, op1=ALU.mult).then_inc(o_evac, 1)
                    if G_LN <= g < G_LN + ST:
                        layer_norm(g - G_LN)
                    h = g - 1
                    if h >= 0 and is_gate(h):
                        gate_ready(half, h)
                        if h < G_UA:
                            if half == 1 and h == G_Q + 1:
                                ve.wait_ge(y_stored, 16 * ST)
                            ve.scalar_tensor_tensor(out=mix[:, (h - G_Q) // 2, :], in0=act[:, 0:HS],
                                                    scalar=1.0, in1=pre[:, 0:HS], op0=ALU.add, op1=ALU.mult
                                                    ).then_inc(gate_used, 1)
                            ve.wait_ge(gate_used, GATES * half + gate_index(h) + 1)
                        elif h < G_GA:
                            j = h - G_UA
                            ve.wait_ge(sgu_ready, 4 * half + j + 1)
                            settle(ve.tensor_tensor(
                                aux[:, 0:HS].rearrange("p (b i) -> p b i", b=4),
                                E[0][:].rearrange("p (b i) -> p b i", b=4),
                                b_s_sb[:, j, :].unsqueeze(1).broadcast_to([P, 4, P]), ALU.add))
                            ve.tensor_tensor(mix[:, M_A + j, :], aux[:, 0:HS], act[:, 0:HS], ALU.mult
                                             ).then_inc(gate_used, 1)
                            ve.wait_ge(gate_used, GATES * half + gate_index(h) + 1)
                        elif h < G_C:
                            j = h - G_GA
                            ve.tensor_tensor(mix[:, M_A + j, :], mix[:, M_A + j, :], act[:, 0:HS], ALU.mult
                                             ).then_inc(gate_used, 1)
                        else:
                            j = (h - G_C) // 2
                            ve.wait_ge(pool_ready, 4 * half + j + 1)
                            ve.scalar_tensor_tensor(out=mix[:, M_C + j, :], in0=E[1][:],
                                                    scalar=c_scale_sb[:, j:j + 1], in1=act[:, 0:HS],
                                                    op0=ALU.mult, op1=ALU.mult).then_inc(gate_used, 1)
                    n = g - 1 - SLOT_S
                    if 0 <= n < PIECES:
                        softmax_norm(half, n)
                    if g == G_OUT - 1:
                        for kt in range(KT - 1):
                            mix_lo(half, kt)
                    if g == G_OUT:
                        mix_lo(half, KT - 1)
                    if half == 0 and g > G_LAST:
                        for kt in range(4 * (g - G_LAST - 1), 4 * (g - G_LAST)):
                            x_lo(1, kt)
            finish_pair(1)

        @block.tensor
        def _(pe):
            def w_tile(part, slot, at, n):
                return part[:, slot, at:at + n]

            def three(psum_out, stat, mov, first, last):
                pe.matmul(psum_out, stat[0], mov[0], start=first, stop=False)
                pe.matmul(psum_out, stat[0], mov[1], start=False, stop=False)
                return pe.matmul(psum_out, stat[1], mov[0], start=False, stop=last)

            def split_ready(G, s):
                pe.wait_ge(lo_done, split_index(G, s) + 1)

            def t_products(half, g, sub):
                G = GROUPS * half + g
                bank = T[t_index(g) % 2]
                split_ready(G, sub)
                for kt in range(8 * sub, 8 * sub + 8):
                    if g == 0:
                        pe.wait_ge(x_lo_done, KT * half + kt + 1)
                    at = P * kt
                    mm = three(bank[:], (w_tile(w_hi, G % 2, at, P), w_tile(w_lo, G % 2, at, P)),
                               (op_hi[:, kt, :], op_lo[:, kt, :]), kt == 0, kt == KT - 1)
                    if g == G_OUT - 1 and kt % 4 == 3 and kt < KT - 1:
                        mm.then_inc(x_read, 1)
                if sub == 1:
                    mm.then_inc(group_done, 1)

            def t_free(half, g):
                n = T_TILES * half + t_index(g)
                if n >= 2:
                    pe.wait_ge(t_evac, n - 1)

            def k_tiles(half):
                t_free(half, 0)
                t_free(half, 1)
                for sub in range(2):
                    for g in range(2):
                        t_products(half, g, sub)

            def t_tile(half, g):
                t_free(half, g)
                for sub in range(2):
                    t_products(half, g, sub)

            def n_group(half, g, width, kts, sts=range(ST)):
                G = GROUPS * half + g
                for k, kt in enumerate(kts):
                    if k % (len(kts) // 2) == 0:
                        split_ready(G, k // (len(kts) // 2))
                    if g >= G_OUT and g < G_OUT + 4:
                        pe.wait_ge(m_lo_done, KT * half + kt + 1)
                    for st in sts:
                        pos = slice(P * st, P * st + P)
                        if kt == 0:
                            n_free(half, g, st)
                        mm = three(N[st][:, 0:width], (op_hi[:, kt, pos], op_lo[:, kt, pos]),
                                   (w_tile(w_hi, G % 2, width * k, width), w_tile(w_lo, G % 2, width * k, width)),
                                   kt == 0, kt == KT - 1)
                        if kt == KT - 1 and st != sts[-1]:
                            mm.then_inc(bank_done[st], 1)
                mm.then_inc(group_done, 1)

            def n_free(half, g, st):
                if g == G_V and half == 1:
                    pe.wait_ge(y_evac, ST * 3 + st + 1)
                if g == G_VA:
                    pe.wait_ge(v_evac, ST * half + st + 1)
                if g == G_OUT:
                    pe.wait_ge(o_evac, PIECES * (half + 1))
                if g > G_OUT:
                    c = min((g - G_OUT) // 4, 3)
                    pe.wait_ge(y_evac, ST * (4 * half + c - 1) + st + 1)

            def scores(half, n):
                i, tp, m = n // 2, n % 2, PIECES * half + n
                pair = i // 4
                pe.wait_ge(t_evac, T_TILES * half + t_index(G_Q + 2 * i) + 1)
                if n == 0:
                    pe.wait_ge(va_evac, ST * (half + 1))
                if m >= 1:
                    pe.wait_ge(shifted, 2 * m)
                for tl in range(2):
                    q0 = P * (2 * tp + tl)
                    k0, at = q0, P * tl
                    heads = [(S_bank[a], slice(64 * a, 64 * a + 64)) for a in range(2)]
                    for bank, h in heads:
                        pe.matmul(bank[:, at:at + 64], q_t[h, q0:q0 + P], k_t[h, pair, k0 + 64:k0 + 128],
                                  start=True, stop=True)
                    for bank, h in heads:
                        pe.matmul(bank[0:64, at + 64:at + 128], q_t[h, q0:q0 + 64],
                                  k_t[h, pair, k0:k0 + 64], start=True, stop=True)
                    for bank, h in heads:
                        mm = pe.matmul(bank[64:128, at + 64:at + 128], q_t[h, q0 + 64:q0 + 128],
                                       k_t[h, pair, k0 + 128:k0 + 192], start=True, stop=True)
                mm.then_inc(s_ready, 1)

            def transpose(half, n):
                m = PIECES * half + n
                pe.wait_ge(p_ready, m + 1)
                if m >= 1:
                    pe.wait_ge(pt_evac, m)
                for b in range(4):
                    mm = pe.transpose(PT_bank[:, P * b:P * b + P], probs[:, P * b:P * b + P], ident[:])
                mm.then_inc(pt_ready, 1)

            def values(half, n):
                i, tp, m = n // 2, n % 2, PIECES * half + n
                pe.wait_ge(pt_evac, m + 1)
                if m >= 1:
                    pe.wait_ge(o_evac, m)
                if n == 0:
                    pe.wait_ge(v_ready, 2 * (half + 1))
                for tl in range(2):
                    st = 2 * tp + tl
                    for a in range(2):
                        kv = 2 * (i // 4) + a
                        d, at = slice(64 * kv, 64 * kv + 64), (2 * a + tl) * P
                        for c, vals in enumerate((v_prev, v)):
                            mm = pe.matmul(O_bank[64 * a:64 * a + 64, P * tl + 64 * c:P * tl + 64 * c + 64],
                                           vals[:, st, d], probs_t[:, at + 64 * c:at + 64 * c + 64],
                                           start=True, stop=True)
                mm.then_inc(o_ready, 1)

            for half in range(HALVES):
                for g in range(GROUPS + 4 * half):
                    if g == 0:
                        k_tiles(half)
                        if half == 0:
                            pe.wait_ge(consts_set, 3)
                            pe.wait_ge(consts_loaded, 16 * 11)
                            pe.matmul(E[0][0:HEADS, 0:REL], rel_sb[:], one_hot_sb[:], start=True, stop=True
                                      ).then_inc(table_done, 1)
                    elif g == 1:
                        pass
                    elif is_t(g):
                        t_tile(half, g)
                    elif g < G_VA:
                        n_group(half, g, 256, range(8 * (g - G_V), 8 * (g - G_V) + 8))
                    elif g < G_Q:
                        n_group(half, g, 512, range(4 * (g - G_VA), 4 * (g - G_VA) + 4))
                    else:
                        k0 = 4 * ((g - G_OUT) % 4)
                        sts = range(ST)
                        if half == 1 and g >= G_LAST:
                            sts = range(2) if g < GROUPS else range(2, ST)
                        n_group(half, g, 512, range(k0, k0 + 4), sts)
                    if g == 2:
                        pe.wait_ge(x_acc_done, (KT - 1) * (half + 1))
                        if half == 0:
                            pe.wait_ge(table_copied, 1)
                        pe.matmul(E[0][:], ones[:], rstd_row[:], start=True, stop=True)
                        for st in range(ST):
                            mm = pe.matmul(E[1][:, st:st + 1], rstd_row[:, P * st:P * st + P], ones[:, 0:1],
                                           start=True, stop=True)
                        mm.then_inc(stats_done, 1)
                    if 0 <= g - SLOT_PV < PIECES:
                        values(half, g - SLOT_PV)
                    if 0 <= g - SLOT_PT < PIECES:
                        transpose(half, g - SLOT_PT)
                    if 0 <= g - SLOT_S < PIECES:
                        scores(half, g - SLOT_S)
                    if G_UA <= g < G_GA:
                        j = g - G_UA
                        pe.wait_ge(ln_done, ST * (half + 1))
                        if j >= 1:
                            pe.wait_ge(gate_used, GATES * half + 8 + j)
                        for st in range(ST):
                            mm = pe.matmul(E[0][:, P * st:P * st + P], mix[:, M_A + j, P * st:P * st + P],
                                           w_s_sb[:, j, :], start=True, stop=True)
                        mm.then_inc(sgu_ready, 1)
                    if G_C <= g < G_OUT and g % 2 == 1:
                        j = (g - G_C) // 2
                        pe.wait_ge(pool_in, 4 * half + j + 1)
                        if j >= 1:
                            pe.wait_ge(gate_used, GATES * half + 16 + j)
                        pe.matmul(E[1][:], w_pool_sb[:, j, :], aux[:, HIST:HIST + HS], start=True, stop=True
                                  ).then_inc(pool_ready, 1)


def t5_bucket(rel):
    nb = REL_BUCKETS // 2
    exact = nb // 2
    n = np.abs(rel)
    large = exact + (np.log(np.maximum(n, 1).astype(np.float32) / exact)
                     / np.float32(math.log(REL_MAX_DIST / exact)) * (nb - exact)).astype(np.int32)
    return (rel > 0).astype(np.int32) * nb + np.where(n < exact, n, np.minimum(large, nb - 1))


def weight_stream(w_in, w_out):
    def tile(cols):
        return w_in[:, cols].reshape(KT, P, P).transpose(1, 0, 2).reshape(1, P, GW)

    def rows(m, at, width):
        part = m[:, at:at + width].reshape(KT, P, width).transpose(1, 0, 2)
        n = GW // width
        return part.reshape(P, KT // n, GW).transpose(1, 0, 2)

    span = lambda a, n: np.arange(a, a + n)
    pair = lambda base, i: np.concatenate([span(base + DH * h, DH) for h in tile_heads(i)])
    parts = [tile(span(2560 + P * p, P)) for p in range(2)]
    parts.append(rows(w_in, 2816, 256))
    parts.append(rows(w_in, 512, 512))
    for i in range(8):
        parts += [tile(pair(1536, i)), tile(pair(3072, i))]
    parts += [tile(span(P * j, P)) for j in range(4)]
    parts += [tile(span(1024 + P * j, P)) for j in range(4)]
    for j in range(4):
        parts += [tile(span(4096 + P * j, P)), tile(span(4608 + P * j, P))]
    order = np.concatenate([pair(512, i) for i in range(8)] + [span(0, 512), span(1536, 512)])
    mixed = w_out[order]
    parts += [rows(mixed, 512 * c, 512) for c in range(4)]
    return np.ascontiguousarray(np.concatenate(parts, axis=0))


def kernel(x, norm_g, w_in, a_ln_g, a_ln_b, a_w_s, a_b_s, b_sinks, rel_bias, c_w_pool, c_scale, w_out, final_g):
    import concourse.bacc as bacc
    from concourse.bass_utils import run_bass_kernel_spmd

    (x, norm_g, w_in, a_ln_g, a_ln_b, a_w_s, a_b_s, b_sinks, rel_bias, c_w_pool, c_scale, w_out, final_g) = (
        np.asarray(a) for a in (x, norm_g, w_in, a_ln_g, a_ln_b, a_w_s, a_b_s, b_sinks, rel_bias, c_w_pool,
                                c_scale, w_out, final_g))
    heads = np.array([h for i in range(8) for h in tile_heads(i)])
    one_hot = (t5_bucket(np.arange(REL) - 127)[None, :] == np.arange(REL_BUCKETS)[:, None]).astype(np.float32)
    counts = np.array([[1.0 / min(t + 1, window) for t in range(HIST)] for window in POOLS], np.float32)
    arrays = {
        "x": x[0],
        "x_t": x[0].T.reshape(4, 4, P, HALVES, HS).transpose(3, 0, 2, 1, 4).reshape(HALVES, 4, P, 4 * HS),
        "w": weight_stream(w_in[0], w_out[0]),
        "norm_g": norm_g[0].reshape(KT, P).T,
        "ln_g": a_ln_g, "ln_b": a_ln_b,
        "w_s": a_w_s[0].transpose(2, 0, 1).reshape(P, 4 * P),
        "b_s": a_b_s[0].reshape(1, 4 * P),
        "sinks": b_sinks[:, heads],
        "rel_bias": rel_bias[:, heads],
        "one_hot": one_hot,
        "inv_count": counts.reshape(1, 4 * HIST),
        "w_pool": c_w_pool[0].transpose(1, 0, 2).reshape(P, 4 * P),
        "c_scale": c_scale[0].reshape(4, P).T,
        "final_g": final_g.reshape(1, D),
    }
    arrays = {f"{k}_dram": np.ascontiguousarray(a) for k, a in arrays.items()}
    nc = bacc.Bacc("TRN2", target_bir_lowering=False, num_devices=1, dynamic_dma_scratch_size=1024)
    args = [nc.dram_tensor(k, a.shape, mybir.dt.from_np(a.dtype), kind="ExternalInput").ap()
            for k, a in arrays.items()]
    out = nc.dram_tensor("out_dram", (SEQ, D), F32, kind="ExternalOutput").ap()
    build(nc, *args, out)
    r = run_bass_kernel_spmd(nc, [arrays], core_ids=[0])
    return r.results[0]["out_dram"].reshape(1, SEQ, D)
```

```python
import math
from contextlib import ExitStack

import numpy as np

import concourse.bass as bass
from concourse import mybir

ALU = mybir.AluOpType
ACT = mybir.ActivationFunctionType
AX = mybir.AxisListType
F32 = mybir.dt.float32
F32R = mybir.dt.float32r

P = 128
SEQ, D = 1024, 2048
HALVES = 2
HS = SEQ // HALVES
ST = HS // P
KT = D // P
CHUNK = 64
HEADS, KV_HEADS, DH = 16, 4, 64
EPS = 1e-6
REL_BUCKETS, REL_MAX_DIST = 32, 128
COLS = 256
REL = 192
WINDOW = 3 * CHUNK
POOLS = (2, 4, 8, 16)
SQUARES_LAG = 6
HIST = 16

G_K, G_V, G_VA, G_Q, G_UA, G_GA, G_C, G_OUT, GROUPS = 0, 2, 4, 8, 24, 28, 32, 40, 56
G_LAST = GROUPS - 4
TOTAL = 2 * GROUPS + 4
N_OUTPUTS = 6
G_LN = G_Q + 4
GW = 2048
PIECES = 16
SLOT_S, SLOT_PT, SLOT_PV = 9, 10, 11
GATES = 20
T_TILES = 34
M_A, M_C = 8, 12


def t_index(g):
    return g if g < G_V else g - G_Q + 2


def gate_index(g):
    if g < G_UA:
        return (g - G_Q) // 2
    if g < G_C:
        return 8 + g - G_UA
    return 16 + (g - G_C) // 2


def is_t(g):
    return g < G_V or G_Q <= g < G_OUT


def is_gate(g):
    return (G_Q <= g < G_UA and g % 2 == 1) or G_UA <= g < G_C or (G_C <= g < G_OUT and g % 2 == 1)


def split_parts(G):
    return 4 if G < 2 else 2


def split_index(G, part):
    return 2 * part + G if G < 2 else 2 * (G - 2) + 8 + part


def x_load(kt):
    return kt if kt < 4 else 4 + (kt - 4) // 2


def wait_loaded(eng, raw_loaded, first_loaded, G, part):
    if G < 2:
        eng.wait_ge(first_loaded[4 * G + part], 16)
    else:
        eng.wait_ge(raw_loaded[G % 2], 16 * (G // 2))


def wait_output(eng, bank_done, group_done, half, u, st):
    end = (G_VA, G_Q, G_OUT + 4, G_OUT + 8, G_OUT + 12, GROUPS)[u]
    if half == 1 and u == N_OUTPUTS - 1:
        last, end = (1, end) if st < 2 else (3, end + 4)
    else:
        last = ST - 1
    if st == last:
        eng.wait_ge(group_done, GROUPS * half + end)
    else:
        eng.wait_ge(bank_done[st], N_OUTPUTS * half + u + 1)


def tile_heads(i):
    return 8 * (i // 4) + i % 4, 8 * (i // 4) + 4 + i % 4


def build(nc, x, x_t, w, norm_g, ln_g, ln_b, w_s, b_s, sinks, rel_bias, one_hot, inv_count, w_pool,
          c_scale, final_g, out):
    table = nc.dram_tensor("rel_table", [CHUNK, HEADS, REL], F32).ap()
    with ExitStack() as ctx:
        def sb(name, shape, dt=F32):
            return ctx.enter_context(nc.sbuf_tensor(name, shape, dt))

        def psum(name):
            return ctx.enter_context(nc.psum_tensor(name, [P, 512], F32))

        def sem(name):
            return ctx.enter_context(nc.semaphore(name))

        op_hi = sb("op_hi", [P, KT, HS], F32R)
        op_lo = sb("op_lo", [P, KT, HS], F32R)
        mix = sb("mix", [P, KT, HS])
        raw = sb("raw", [P, 2, GW])
        w_hi = sb("w_hi", [P, 2, GW], F32R)
        w_lo = sb("w_lo", [P, 2, GW], F32R)
        x_raw = sb("x_raw", [P, 2, HS])
        x_sq = sb("x_sq", [P, 2, HS])
        rstd_row = sb("rstd_row", [P, HS])
        k_hi = sb("k_hi", [P, KV_HEADS, CHUNK + HS], F32R)
        k_lo = sb("k_lo", [P, KV_HEADS, CHUNK + HS], F32R)
        v = sb("v", [P, ST, KV_HEADS * DH])
        v_prev = sb("v_prev", [P, ST, KV_HEADS * DH])
        probs = sb("probs", [P, HIST + HS])
        probs_t = sb("probs_t", [P, HIST + HS])
        q_t = sb("q_t", [P, HIST + HS])
        q_stack = sb("q_stack", [P, 2, HS], F32R)
        aux = sb("aux", [P, HIST + HS])
        norm_g_sb = sb("norm_g_sb", [P, KT])
        ln_g_sb = sb("ln_g_sb", [P, 512])
        ln_b_sb = sb("ln_b_sb", [P, 512])
        w_s_sb = sb("w_s_sb", [P, 4, P])
        b_s_sb = sb("b_s_sb", [P, 4, P])
        sink_sb = sb("sink_sb", [P, HEADS])
        rel_sb = sb("rel_sb", [REL_BUCKETS, HEADS])
        one_hot_sb = sb("one_hot_sb", [REL_BUCKETS, REL])
        table_sb = sb("table_sb", [HEADS, REL])
        bias = sb("bias", [P, HEADS, P])
        inv_sb = sb("inv_sb", [P, 4, HIST])
        w_pool_sb = sb("w_pool_sb", [P, 4, P])
        c_scale_sb = sb("c_scale_sb", [P, 4])
        final_g_sb = sb("final_g_sb", [P, D])
        ones = sb("ones", [P, P])
        ident = sb("ident", [P, P])
        hist = sb("hist", [P, 4, HIST])
        head_sum = sb("head_sum", [P, HIST])
        eps_sb = sb("eps_sb", [P, 1])
        root_row = sb("root_row", [P, 4])
        rstd_col = sb("rstd_col", [P, 4])
        root_ln = sb("root_ln", [P, 4])
        rstd_ln = sb("rstd_ln", [P, 4])
        bn = sb("bn", [P, 4, 6])
        mean_var = sb("mean_var", [P, 4, 2])
        row_max = sb("row_max", [P, 4])
        sink_d = sb("sink_d", [P, 4])
        sink_e = sb("sink_e", [P, 4])
        row_sum = sb("row_sum", [P, 4])
        row_inv = sb("row_inv", [P, 4])
        ssq = sb("ssq", [P, ST, 4])
        ssq_sum = sb("ssq_sum", [P, ST])
        root_y = sb("root_y", [P, ST])
        rstd_y = sb("rstd_y", [P, ST])
        pre, act = x_raw[:, 0, :], x_sq[:, 0, :]
        k_stage = (q_t, pre)
        residual = [probs, probs_t, q_t, aux]

        T = [psum(f"t_bank{i}") for i in range(2)]
        N = [psum(f"n_bank{i}") for i in range(4)]
        E = [psum(f"e_bank{i}") for i in range(2)]
        S_bank, PT_bank, O_bank = (N[0], N[3]), N[1], N[2]

        act_warm = sem("act_warm")
        raw_loaded = [sem(f"raw_loaded{i}") for i in range(2)]
        first_loaded = [sem(f"first_loaded{i}") for i in range(8)]
        hi_done, lo_done, group_done = sem("hi_done"), sem("lo_done"), sem("group_done")
        norm_g_loaded = sem("norm_g_loaded")
        x_loaded = [sem(f"x_loaded{i}") for i in range(x_load(KT - 1) + 1)]
        x_raw_loaded = [sem(f"x_raw_loaded{i}") for i in range(2)]
        bank_done = [sem(f"bank_done{i}") for i in range(ST)]
        x_hi_done, x_lo_done, x_sq_done, x_acc_done = (sem("x_hi_done"), sem("x_lo_done"), sem("x_sq_done"),
                                                       sem("x_acc_done"))
        x_read = sem("x_read")
        m_hi_done, m_lo_done = sem("m_hi_done"), sem("m_lo_done")
        consts_loaded, consts_set = sem("consts_loaded"), sem("consts_set")
        table_copied, table_stored, bias_loaded = sem("table_copied"), sem("table_stored"), sem("bias_loaded")
        stats_done, root_done, rstd_done = sem("stats_done"), sem("root_done"), sem("rstd_done")
        t_evac, v_evac, v_saved, va_evac = sem("t_evac"), sem("v_evac"), sem("v_saved"), sem("va_evac")
        v_ready = sem("v_ready")
        ln_var, ln_root, ln_done = sem("ln_var"), sem("ln_root"), sem("ln_done")
        q_hi_done, q_lo_done, k_hi_done, k_lo_done = (sem("q_hi_done"), sem("q_lo_done"), sem("k_hi_done"),
                                                      sem("k_lo_done"))
        k_saved = sem("k_saved")
        s_ready, shifted, exp_done, p_ready = sem("s_ready"), sem("shifted"), sem("exp_done"), sem("p_ready")
        pt_ready, pt_evac, o_ready, o_evac = sem("pt_ready"), sem("pt_evac"), sem("o_ready"), sem("o_evac")
        gate_fn, gate_used = sem("gate_fn"), sem("gate_used")
        sgu_ready, pool_in, pool_ready = sem("sgu_ready"), sem("pool_in"), sem("pool_ready")
        res_loaded = [sem(f"res_loaded{i}") for i in range(ST)]
        ssq_done, ssq_summed = sem("ssq_done"), sem("ssq_summed")
        y_evac, y_root, y_inverted = sem("y_evac"), sem("y_root"), sem("y_inverted")
        y_scaled, y_normed, y_stored = sem("y_scaled"), sem("y_normed"), sem("y_stored")
        dve_settled, pool_settled = sem("dve_settled"), sem("pool_settled")

        block = ctx.enter_context(nc.Block())

        @block.sync
        def _(sp):
            def store(half, st):
                s0 = HS * half + P * st
                if half == 0:
                    sp.wait_ge(y_normed, st + 1)
                else:
                    sp.wait_ge(y_normed, ST + 2 * st + 2)
                    sp.wait_ge(y_scaled, 2 * st + 2)
                sp.dma_start(out[s0:s0 + P, :], mix[:, 4 * st:4 * st + 4, :].rearrange("p c d -> p (c d)")
                             ).then_inc(y_stored, 16)

            def store_last():
                st = ST - 1
                for c, done, count in ((2, y_normed, ST + 2 * st + 1), (0, y_scaled, 2 * st + 1),
                                       (3, y_normed, ST + 2 * st + 2), (1, y_scaled, 2 * st + 2)):
                    sp.wait_ge(done, count)
                    sp.dma_start(out[SEQ - P:SEQ, 512 * c:512 * c + 512], mix[:, 4 * st + c, :]
                                 ).then_inc(y_stored, 16)

            def load_group(G):
                sp.wait_ge(lo_done, split_index(G - 2, split_parts(G - 2) - 1) + 1)
                g = G % GROUPS if G < 2 * GROUPS else G % GROUPS + G_LAST
                sp.dma_start(raw[:, G % 2, :], w[g]).then_inc(raw_loaded[G % 2], 16)

            def load_first(G, part):
                sp.dma_start(raw[:, G, 512 * part:512 * part + 512], w[G, :, 512 * part:512 * part + 512]
                             ).then_inc(first_loaded[4 * G + part], 16)

            def load_x(kt, n):
                sp.dma_start(mix[:, kt:kt + n, :].rearrange("p k s -> p (k s)"),
                             x_t[0, kt // 4, :, HS * (kt % 4):HS * (kt % 4 + n)]).then_inc(x_loaded[x_load(kt)], 16)

            def rows(a, n):
                return bass.AP(a.tensor, 0, [[0, P], [1, n]])

            def load_constants():
                for dst, src in ((rel_sb[:], rel_bias), (one_hot_sb[:], one_hot), (sink_sb[:], rows(sinks, HEADS)),
                                 (ln_g_sb[:], rows(ln_g, 512)), (ln_b_sb[:], rows(ln_b, 512)),
                                 (w_s_sb[:].rearrange("p g i -> p (g i)"), w_s),
                                 (b_s_sb[:].rearrange("p g i -> p (g i)"), rows(b_s, 512)),
                                 (inv_sb[:].rearrange("p g i -> p (g i)"), rows(inv_count, 4 * HIST)),
                                 (w_pool_sb[:].rearrange("p g i -> p (g i)"), w_pool), (c_scale_sb[:], c_scale),
                                 (final_g_sb[:], rows(final_g, D))):
                    sp.dma_start(dst, src).then_inc(consts_loaded, 16)

            load_first(0, 0)
            sp.dma_start(norm_g_sb[:], norm_g).then_inc(norm_g_loaded, 16)
            for part in range(4):
                if part > 0:
                    load_first(0, part)
                n = 1 if part == 0 else 2
                for kt in range(4 * part, 4 * part + 4, n):
                    load_x(kt, n)
                load_first(1, part)

            for half in range(HALVES):
                for g in range(GROUPS + 4 * half):
                    G = GROUPS * half + g
                    if G + 2 < TOTAL:
                        load_group(G + 2)
                    if half == 0 and g == 1:
                        load_constants()
                    if half == 0 and g == G_VA:
                        sp.wait_ge(table_copied, 1)
                        sp.dma_start(table.rearrange("q h r -> h q r"),
                                     table_sb[:].unsqueeze(1).broadcast_to([HEADS, CHUNK, REL])).then_inc(table_stored, 16)
                        sp.wait_ge(table_stored, 16)
                        for q0 in (0, CHUNK):
                            sp.dma_start(bias[q0:q0 + CHUNK, :, :],
                                         bass.AP(table.tensor, 127 - CHUNK, [[HEADS * REL - 1, CHUNK], [REL, HEADS], [1, P]])
                                         ).then_inc(bias_loaded, 16)
                    if G_OUT <= g < GROUPS and g % 4 == 1:
                        c = (g - G_OUT) // 4
                        n = 4 * half + c
                        if c == 0:
                            sp.wait_ge(m_lo_done, KT * (half + 1))
                        else:
                            sp.wait_ge(y_evac, ST * n)
                        for st in range(ST):
                            s0 = HS * half + P * st
                            sp.dma_start(residual[st][:, 0:512], x[s0:s0 + P, 512 * c:512 * c + 512]
                                         ).then_inc(res_loaded[st], 16)
                    if half == 0 and g >= G_LAST:
                        for kt in range(4 * (g - G_LAST), 4 * (g - G_LAST) + 4):
                            if kt >= 2:
                                sp.wait_ge(x_lo_done, KT + kt - 1)
                                sp.wait_ge(x_sq_done, KT + kt - 1)
                            sp.dma_start(x_raw[:, kt % 2, :], x_t[1, kt // 4, :, HS * (kt % 4):HS * (kt % 4) + HS]
                                         ).then_inc(x_raw_loaded[kt % 2], 16)
                    if half == 1 and 1 <= g <= ST:
                        store(0, g - 1)
            for st in range(ST - 1):
                store(1, st)
            store_last()
            sp.wait_ge(y_stored, 16 * (2 * ST - 1 + 4))

        @block.gpsimd
        def _(pool):
            settled = [0]

            def settle(ins):
                settled[0] += 1
                ins.then_inc(pool_settled, 1)
                pool.wait_ge(pool_settled, settled[0])

            pool.memset(ones[:], 1.0).then_inc(consts_set, 1)
            pool.memset(eps_sb[:], EPS).then_inc(consts_set, 1)
            settle(pool.memset(ident[:], 0.0))
            pool.affine_select(out=ident[:], in_=ident[:], compare_op=ALU.not_equal, fill=1.0, base=0,
                               pattern=[[-1, P]], channel_multiplier=1).then_inc(consts_set, 1)

            for half in range(HALVES):
                for kt in range(1, KT):
                    pool.wait_ge(x_sq_done, KT * half + kt + 1)
                    pool.tensor_tensor(rstd_row[:], rstd_row[:], x_sq[:, kt % 2, :], ALU.add
                                       ).then_inc(x_acc_done, 1)
                    pool.wait_ge(x_acc_done, (KT - 1) * half + kt)

        @block.scalar
        def _(sc):
            def square_y(half, c, sts=range(ST)):
                for st in sts:
                    n = ST * (4 * half + c) + st
                    sc.wait_ge(y_evac, n + 1)
                    if n >= 1:
                        sc.wait_ge(ssq_done, n)
                    sc.activation(E[1][:], mix[:, 4 * st + c, :], ACT.Square,
                                  accum_out=ssq[:, st, c:c + 1]).then_inc(ssq_done, 1)

            def root_of_y(half):
                sc.wait_ge(ssq_summed, half + 1)
                sc.activation(root_y[:], ssq_sum[:], ACT.Sqrt, bias=eps_sb[:], scale=1.0 / D
                              ).then_inc(y_root, 1)

            def finish(st):
                col = slice(st, st + 1)
                sc.wait_ge(ssq_summed, 2 + st)
                sc.activation(root_y[:, col], ssq_sum[:, col], ACT.Sqrt, bias=eps_sb[:], scale=1.0 / D
                              ).then_inc(y_root, 1)
                sc.wait_ge(y_inverted, 2 + st)
                for c in range(2):
                    tile = mix[:, 4 * st + c, :]
                    sc.activation(tile, tile, ACT.Copy, scale=rstd_y[:, col]).then_inc(y_scaled, 1)

            def split_hi(G, parts=(0, 1)):
                for part in parts:
                    wait_loaded(sc, raw_loaded, first_loaded, G, part)
                    if G >= 2:
                        sc.wait_ge(group_done, G - 1)
                    width = GW // split_parts(G)
                    part = slice(width * part, width * part + width)
                    sc.activation(w_hi[:, G % 2, part], raw[:, G % 2, part], ACT.Copy).then_inc(hi_done, 1)

            def x_tile(half, kt):
                return mix[:, kt, :] if half == 0 else x_raw[:, kt % 2, :]

            def x_hi(half, kt):
                if half == 0:
                    sc.wait_ge(x_loaded[x_load(kt)], 16)
                else:
                    sc.wait_ge(x_raw_loaded[kt % 2], 16 * (kt // 2 + 1))
                    sc.wait_ge(group_done, G_LAST + kt // 4 + 1)
                sc.activation(op_hi[:, kt, :], x_tile(half, kt), ACT.Copy, scale=norm_g_sb[:, kt:kt + 1]
                              ).then_inc(x_hi_done, 1)

            def x_square(half, kt):
                src = x_tile(half, kt)
                if kt == 0:
                    if half == 1:
                        sc.wait_ge(t_evac, T_TILES)
                    sc.activation(rstd_row[:], src, ACT.Square).then_inc(x_sq_done, 1)
                else:
                    if kt >= 3:
                        sc.wait_ge(x_acc_done, (KT - 1) * half + kt - 2)
                    sc.activation(x_sq[:, kt % 2, :], src, ACT.Square).then_inc(x_sq_done, 1)

            def k_tile_hi(half, pair):
                if half == 1:
                    sc.wait_ge(k_saved, 2)
                sc.wait_ge(t_evac, T_TILES * half + pair + 1)
                for a in range(2):
                    for to in (a, 1 - a):
                        sc.activation(k_hi[64 * to:64 * to + 64, 2 * pair + a, CHUNK:CHUNK + HS],
                                      k_stage[pair][64 * a:64 * a + 64, 0:HS], ACT.Copy).then_inc(k_hi_done, 1)

            def q_tile_hi(half, i):
                n = 8 * half + i
                sc.wait_ge(t_evac, T_TILES * half + t_index(G_Q + 2 * i) + 1)
                if n >= 1:
                    sc.wait_ge(s_ready, 2 * n)
                for a in range(2):
                    rows = slice(64 * a, 64 * a + 64)
                    sc.activation(q_stack[rows, a, :], q_t[rows, 0:HS], ACT.Copy).then_inc(q_hi_done, 1)

            def mix_hi(half, kt):
                if kt < 12:
                    sc.wait_ge(x_read, 3 * half + kt // 4 + 1)
                else:
                    sc.wait_ge(group_done, GROUPS * half + G_OUT)
                sc.wait_ge(gate_used, GATES * (half + 1) - (1 if kt < KT - 1 else 0))
                sc.activation(op_hi[:, kt, :], mix[:, kt, :], ACT.Copy).then_inc(m_hi_done, 1)

            sc.wait_ge(consts_set, 1)
            sc.activation(root_ln[:], ones[:, 0:4], ACT.Copy).then_inc(act_warm, 1)
            for part in range(4):
                split_hi(0, (part,))
                if part == 0:
                    sc.wait_ge(norm_g_loaded, 16)
                for kt in range(4 * part, 4 * part + 4):
                    x_hi(0, kt)
                    if kt >= SQUARES_LAG:
                        x_square(0, kt - SQUARES_LAG)
                split_hi(1, (part,))
            sc.wait_ge(consts_set, 3)
            for half in range(HALVES):
                for g in range(GROUPS + 4 * half):
                    G = GROUPS * half + g
                    if g == G_VA:
                        sc.wait_ge(v_saved, half + 1)
                        for st in range(ST):
                            wait_output(sc, bank_done, group_done, half, 0, st)
                            sc.activation(v[:, st, :], N[st][:, 0:256], ACT.Copy, scale=rstd_col[:, st:st + 1]
                                          ).then_inc(v_evac, 1)
                    if g == G_Q:
                        if half == 1:
                            sc.wait_ge(y_stored, 16 * ST)
                        for st in range(ST):
                            wait_output(sc, bank_done, group_done, half, 1, st)
                            sc.activation(mix[:, M_A:M_A + 4, P * st:P * st + P],
                                          N[st][:].rearrange("p (j d) -> p j d", j=4), ACT.Gelu,
                                          scale=rstd_col[:, st:st + 1]).then_inc(va_evac, 1)
                    if 2 <= G + 1 < TOTAL:
                        split_hi(G + 1)
                    if half == 1 and g == 0:
                        for kt in range(12, KT):
                            x_hi(1, kt)
                            x_square(1, kt)
                    if half == 0 and g == 1:
                        for kt in range(KT - SQUARES_LAG, KT):
                            x_square(0, kt)
                    if g == G_V + 1:
                        sc.wait_ge(stats_done, half + 1)
                        if half == 0:
                            sc.activation(table_sb[:], E[0][0:HEADS, 0:REL], ACT.Copy).then_inc(table_copied, 1)
                        sc.activation(root_row[:], E[0][:, COLS:COLS + ST], ACT.Sqrt, bias=eps_sb[:], scale=1.0 / D
                                      ).then_inc(root_done, 1)
                        sc.activation(rstd_row[:], E[1][:], ACT.Sqrt, bias=eps_sb[:], scale=1.0 / D
                                      ).then_inc(root_done, 1)
                    if g == G_LN - 1:
                        sc.wait_ge(ln_var, half + 1)
                        sc.activation(root_ln[:], mean_var[:, :, 1], ACT.Sqrt, bias=eps_sb[:]
                                      ).then_inc(ln_root, 1)
                    if g >= 1 and is_gate(g - 1):
                        n = GATES * half + gate_index(g - 1)
                        sc.wait_ge(t_evac, T_TILES * half + t_index(g - 1) + 1)
                        if n >= 1:
                            sc.wait_ge(gate_used, n)
                        if g - 1 < G_UA:
                            sc.activation(act[:, 0:HS], pre[:, 0:HS], ACT.Tanh, scale=0.5).then_inc(gate_fn, 1)
                        else:
                            sc.activation(act[:, 0:HS], pre[:, 0:HS], ACT.Gelu if g - 1 < G_GA else ACT.Silu
                                          ).then_inc(gate_fn, 1)
                    if g in (G_VA, G_VA + 1):
                        k_tile_hi(half, g - G_VA)
                    if G_Q <= g - 1 < G_UA and (g - 1 - G_Q) % 2 == 0:
                        q_tile_hi(half, (g - 1 - G_Q) // 2)
                    n = g - 1 - SLOT_PT
                    if 0 <= n < PIECES:
                        m = PIECES * half + n
                        sc.wait_ge(pt_ready, m + 1)
                        if m >= 1:
                            sc.wait_ge(o_ready, m)
                        sc.activation(probs_t[:, 0:512], PT_bank[:], ACT.Copy).then_inc(pt_evac, 1)
                    n = g - 1 - SLOT_S
                    if 0 <= n < PIECES:
                        m = PIECES * half + n
                        sc.wait_ge(shifted, 2 * m + 2)
                        sc.activation(sink_e[:], sink_d[:], ACT.Exp).then_inc(exp_done, 1)
                        sc.activation(probs[:, 0:512], probs[:, 0:512], ACT.Exp).then_inc(exp_done, 1)
                    if g == G_OUT - 1:
                        for kt in range(KT - 1):
                            mix_hi(half, kt)
                    if g == G_OUT:
                        mix_hi(half, KT - 1)
                    if G_OUT + 4 <= g < GROUPS and g % 4 == 0:
                        square_y(half, (g - G_OUT) // 4 - 1)
                    if half == 1 and g == 0:
                        square_y(0, 3)
                        root_of_y(0)
                    if half == 1 and g == GROUPS:
                        square_y(1, 3, range(2))
                    if half == 1 and g > GROUPS and g < GROUPS + 3:
                        finish(g - GROUPS - 1)
                    if half == 0 and g > G_LAST:
                        for kt in range(4 * (g - G_LAST - 1), 4 * (g - G_LAST)):
                            x_hi(1, kt)
                            x_square(1, kt)
            for st in range(2, ST):
                square_y(1, 3, (st,))
                finish(st)

        @block.vector
        def _(ve):
            settled = [0]

            def settle(ins):
                settled[0] += 1
                ins.then_inc(dve_settled, 1)
                ve.wait_ge(dve_settled, settled[0])

            def split_lo(G, parts=(0, 1)):
                for part in parts:
                    ve.wait_ge(hi_done, split_index(G, part) + 1)
                    width = GW // split_parts(G)
                    part = slice(width * part, width * part + width)
                    ve.tensor_tensor(w_lo[:, G % 2, part], raw[:, G % 2, part], w_hi[:, G % 2, part].bitcast(F32),
                                     ALU.subtract).then_inc(lo_done, 1)

            def x_lo(half, kt):
                src = mix[:, kt, :] if half == 0 else x_raw[:, kt % 2, :]
                ve.wait_ge(x_hi_done, KT * half + kt + 1)
                ve.scalar_tensor_tensor(out=op_lo[:, kt, :], in0=src, scalar=norm_g_sb[:, kt:kt + 1],
                                        in1=op_hi[:, kt, :].bitcast(F32), op0=ALU.mult, op1=ALU.subtract
                                        ).then_inc(x_lo_done, 1)

            def mix_lo(half, kt):
                ve.wait_ge(m_hi_done, KT * half + kt + 1)
                ve.tensor_tensor(op_lo[:, kt, :], mix[:, kt, :], op_hi[:, kt, :].bitcast(F32), ALU.subtract
                                 ).then_inc(m_lo_done, 1)

            def take(half, g, dst):
                ve.tensor_tensor(dst, T[t_index(g) % 2][:], rstd_row[:], ALU.mult).then_inc(t_evac, 1)
                ve.wait_ge(t_evac, T_TILES * half + t_index(g) + 1)

            def gate_ready(half, g):
                ve.wait_ge(gate_fn, GATES * half + gate_index(g) + 1)

            def softmax_scores(half, n):
                i, tp, m = n // 2, n % 2, PIECES * half + n
                ve.wait_ge(s_ready, m + 1)
                if m == 0:
                    ve.wait_ge(bias_loaded, 32)
                for c in range(2):
                    rows = slice(64 * c, 64 * c + 64)
                    for a in range(2):
                        last = ve.scalar_tensor_tensor(
                            out=probs[rows, 256 * a:256 * a + 256].rearrange("p (t s) -> p t s", t=2),
                            in0=S_bank[a][rows, 0:2 * WINDOW].rearrange("p (t s) -> p t s", t=2)[:, :, 64 * c:64 * c + P],
                            scalar=DH ** -0.5, in1=bias[rows, 2 * i + a, :].unsqueeze(1).broadcast_to([64, 2, P]),
                            op0=ALU.mult, op1=ALU.add)
                settle(last)
                if half == 0 and tp == 0:
                    off = probs[0:64, 0:512].rearrange("p (h t s) -> p h t s", h=2, t=2)[:, :, 0, 0:64]
                    settle(ve.memset(off, -1e30))
                scores = probs[:, 0:512].rearrange("p (b s) -> p b s", b=4)
                sink4 = sink_sb[:, 2 * i:2 * i + 2].unsqueeze(2).broadcast_to([P, 2, 2])
                settle(ve.tensor_reduce(row_max[:], scores, AX.X, ALU.max))
                settle(ve.tensor_tensor(row_max[:].rearrange("p (h t) -> p h t", h=2),
                                        row_max[:].rearrange("p (h t) -> p h t", h=2), sink4, ALU.max))
                ve.tensor_tensor(sink_d[:].rearrange("p (h t) -> p h t", h=2), sink4,
                                 row_max[:].rearrange("p (h t) -> p h t", h=2), ALU.subtract
                                 ).then_inc(shifted, 1)
                ve.tensor_tensor(scores, scores, row_max[:].unsqueeze(2).broadcast_to([P, 4, P]),
                                 ALU.subtract).then_inc(shifted, 1)

            def k_tile_lo(half, pair):
                for a in range(2):
                    own = slice(64 * a, 64 * a + 64)
                    ve.wait_ge(k_hi_done, 8 * half + 4 * pair + 2 * a + 1)
                    for to in (a, 1 - a):
                        ve.tensor_tensor(k_lo[64 * to:64 * to + 64, 2 * pair + a, CHUNK:CHUNK + HS],
                                         k_stage[pair][own, 0:HS],
                                         k_hi[own, 2 * pair + a, CHUNK:CHUNK + HS].bitcast(F32),
                                         ALU.subtract).then_inc(k_lo_done, 1)

            def q_tile_lo(half, i):
                for a in range(2):
                    ve.wait_ge(q_hi_done, 16 * half + 2 * i + a + 1)
                    own, other = slice(64 * a, 64 * a + 64), slice(64 - 64 * a, 128 - 64 * a)
                    ve.tensor_tensor(q_stack[other, a, :], q_t[own, 0:HS], q_stack[own, a, :].bitcast(F32),
                                     ALU.subtract).then_inc(q_lo_done, 1)

            def softmax_norm(half, n):
                m = PIECES * half + n
                ve.wait_ge(exp_done, 2 * m + 2)
                scores = probs[:, 0:512].rearrange("p (b s) -> p b s", b=4)
                settle(ve.tensor_reduce(row_sum[:], scores, AX.X, ALU.add))
                settle(ve.tensor_tensor(row_sum[:], row_sum[:], sink_e[:], ALU.add))
                settle(ve.reciprocal(row_inv[:], row_sum[:]))
                ve.tensor_tensor(scores, scores, row_inv[:].unsqueeze(2).broadcast_to([P, 4, P]),
                                 ALU.mult).then_inc(p_ready, 1)

            def layer_norm(st):
                view = mix[:, M_A:M_A + 4, P * st:P * st + P]
                settle(ve.tensor_scalar(view, view, mean_var[:, st, 0:1], rstd_ln[:, st:st + 1],
                                        ALU.subtract, ALU.mult))
                settle(ve.tensor_tensor(view, view, ln_g_sb[:].rearrange("p (j d) -> p j d", j=4), ALU.mult))
                ve.tensor_tensor(view, view, ln_b_sb[:].rearrange("p (j d) -> p j d", j=4), ALU.add
                                 ).then_inc(ln_done, 1)

            def pool_means(half, j):
                window = POOLS[j]
                bufs, src = (probs_t, q_t), probs
                for m in range(j + 1):
                    lo, by, dst = 2 ** (m + 1) - 1, 2 ** m, bufs[m % 2]
                    settle(ve.tensor_tensor(dst[:, lo:HIST + HS], src[:, lo:HIST + HS],
                                            src[:, lo - by:HIST + HS - by], ALU.add))
                    src = dst
                last = ve.scalar_tensor_tensor(out=aux[:, HIST:HIST + HS], in0=src[:, HIST:HIST + HS],
                                               scalar=1.0 / window, in1=probs[:, HIST:HIST + HS],
                                               op0=ALU.mult, op1=ALU.subtract)
                if half == 0:
                    settle(last)
                    settle(ve.tensor_tensor(head_sum[:], src[:, HIST:2 * HIST], inv_sb[:, j, :], ALU.mult))
                    last = ve.tensor_tensor(aux[:, HIST:2 * HIST], head_sum[:], probs[:, HIST:2 * HIST],
                                            ALU.subtract)
                last.then_inc(pool_in, 1)

            def take_y(half, c, sts=range(ST)):
                for st in sts:
                    wait_output(ve, bank_done, group_done, half, 2 + c, st)
                    ve.wait_ge(res_loaded[st], 16 * (4 * half + c + 1))
                    ve.tensor_tensor(mix[:, 4 * st + c, :], N[st][:], residual[st][:, 0:512], ALU.add
                                     ).then_inc(y_evac, 1)

            def sum_ssq():
                ve.wait_ge(ssq_done, 16)
                ve.tensor_reduce(ssq_sum[:], ssq[:], AX.X, ALU.add).then_inc(ssq_summed, 1)

            def norm_y(st):
                if st == 0:
                    ve.wait_ge(y_root, 1)
                    ve.reciprocal(rstd_y[:], root_y[:]).then_inc(y_inverted, 1)
                    ve.wait_ge(y_inverted, 1)
                row = mix[:, 4 * st:4 * st + 4, :].rearrange("p c d -> p (c d)")
                ve.scalar_tensor_tensor(out=row, in0=row, scalar=rstd_y[:, st:st + 1], in1=final_g_sb[:],
                                        op0=ALU.mult, op1=ALU.mult).then_inc(y_normed, 1)

            def weigh_y(c):
                ve.wait_ge(ssq_done, 16 + 4 * c + 4)
                for st in range(ST):
                    tile = mix[:, 4 * st + c, :]
                    settle(ve.tensor_tensor(tile, tile, final_g_sb[:, 512 * c:512 * c + 512], ALU.mult))

            def finish_sum(st):
                ve.wait_ge(ssq_done, 29 + st)
                ve.tensor_reduce(ssq_sum[:, st:st + 1], ssq[:, st, :], AX.X, ALU.add).then_inc(ssq_summed, 1)

            def finish(st):
                ve.wait_ge(y_root, 2 + st)
                ve.reciprocal(rstd_y[:, st:st + 1], root_y[:, st:st + 1]).then_inc(y_inverted, 1)
                ve.wait_ge(y_inverted, 2 + st)
                tile = mix[:, 4 * st + 2, :]
                ve.tensor_scalar(tile, tile, rstd_y[:, st:st + 1], None, ALU.mult).then_inc(y_normed, 1)
                tile = mix[:, 4 * st + 3, :]
                ve.scalar_tensor_tensor(out=tile, in0=tile, scalar=rstd_y[:, st:st + 1],
                                        in1=final_g_sb[:, 1536:2048], op0=ALU.mult, op1=ALU.mult
                                        ).then_inc(y_normed, 1)

            ve.memset(k_hi[:, :, 0:CHUNK].bitcast(F32), 0.0)
            ve.memset(k_lo[:, :, 0:CHUNK].bitcast(F32), 0.0)
            ve.memset(v_prev[:], 0.0)
            settle(ve.memset(hist[:], 0.0))
            for part in range(4):
                split_lo(0, (part,))
                if part == 0:
                    ve.wait_ge(norm_g_loaded, 16)
                for kt in range(4 * part, 4 * part + 4):
                    x_lo(0, kt)
                split_lo(1, (part,))

            for half in range(HALVES):
                for g in range(GROUPS + 4 * half):
                    G = GROUPS * half + g
                    if G_OUT + 4 <= g < GROUPS and g % 4 == 0:
                        take_y(half, (g - G_OUT) // 4 - 1)
                    if half == 1 and g == 0:
                        take_y(0, 3)
                    if half == 1 and g == GROUPS:
                        take_y(1, 3, range(2))
                    if 2 <= G + 1 < TOTAL:
                        split_lo(G + 1)
                    if half == 1 and g == GROUPS:
                        for st in range(2):
                            finish_sum(st)
                    if half == 1 and g > GROUPS and g < GROUPS + 3:
                        finish(g - GROUPS - 1)
                    if half == 1 and g == 0:
                        for kt in range(12, KT):
                            x_lo(1, kt)
                        sum_ssq()
                    if half == 1 and 1 <= g <= ST:
                        norm_y(g - 1)
                    if half == 1 and g in (G_OUT + 6, G_OUT + 10, G_OUT + 14):
                        weigh_y((g - G_OUT - 6) // 4)
                    if g == G_V + 1 and half == 0:
                        ve.wait_ge(consts_loaded, 16 * 11)
                        settle(ve.memset(w_s_sb[64:128, :, 0:64], 0.0))
                    if g == 1 and half == 1:
                        for part in (k_hi, k_lo):
                            ve.tensor_copy(part[:, :, 0:CHUNK], part[:, :, HS:HS + CHUNK].bitcast(F32)
                                           ).then_inc(k_saved, 1)
                    if g == G_V + 1:
                        ve.wait_ge(root_done, 2 * half + 1)
                        ve.reciprocal(rstd_col[:], root_row[:]).then_inc(rstd_done, 1)
                        ve.wait_ge(root_done, 2 * half + 2)
                        ve.reciprocal(rstd_row[:], rstd_row[:]).then_inc(rstd_done, 1)
                        ve.wait_ge(rstd_done, 2 * half + 2)
                        if half == 1:
                            ve.tensor_copy(v_prev[0:64, 0, :], v[64:128, ST - 1, :]).then_inc(v_saved, 1)
                        else:
                            ve.memset(v_prev[0:64, 0, :], 0.0).then_inc(v_saved, 1)
                    if g in (G_VA, G_VA + 1):
                        take(half, g - G_VA, k_stage[g - G_VA][:, 0:HS])
                        k_tile_lo(half, g - G_VA)
                    if g == G_VA:
                        ve.wait_ge(v_evac, ST * (half + 1))
                        ve.tensor_copy(v_prev[64:128, :, :], v[0:64, :, :]).then_inc(v_ready, 1)
                        ve.tensor_copy(v_prev[0:64, 1:ST, :], v[64:128, 0:ST - 1, :]).then_inc(v_ready, 1)
                    if g == G_Q:
                        for st in range(ST):
                            ve.wait_ge(va_evac, ST * half + st + 1)
                            for_stats = mix[:, M_A:M_A + 4, P * st:P * st + P]
                            settle(ve.bn_stats(bn[:, st, :], for_stats))
                            last = ve.bn_aggr(mean_var[:, st, :], bn[:, st, :])
                            if st < ST - 1:
                                settle(last)
                            else:
                                last.then_inc(ln_var, 1)
                    if g == G_LN:
                        ve.wait_ge(ln_root, half + 1)
                        settle(ve.reciprocal(rstd_ln[:], root_ln[:]))
                    if g > G_Q and is_t(g - 1):
                        h = g - 1
                        ve.wait_ge(group_done, G)
                        if h < G_UA and h % 2 == 0:
                            take(half, h, q_t[:, 0:HS])
                        elif G_C <= h and h % 2 == 0:
                            j = (h - G_C) // 2
                            settle(ve.tensor_copy(probs[:, 0:HIST], hist[:, j, :]))
                            take(half, h, probs[:, HIST:HIST + HS])
                            settle(ve.tensor_copy(hist[:, j, :], probs[:, HS:HS + HIST]))
                            if j == 0:
                                ve.wait_ge(o_ready, PIECES * (half + 1))
                            else:
                                ve.wait_ge(pool_ready, 4 * half + j)
                            pool_means(half, j)
                        else:
                            take(half, h, pre[:, 0:HS])
                    n = g - 1 - SLOT_S
                    if 0 <= n < PIECES:
                        softmax_scores(half, n)
                    if G_Q <= g - 1 < G_UA and (g - 1 - G_Q) % 2 == 0:
                        q_tile_lo(half, (g - 1 - G_Q) // 2)
                    n = g - 1 - SLOT_PV
                    if 0 <= n < PIECES:
                        m = PIECES * half + n
                        part = mix[:, n // 2, 256 * (n % 2):256 * (n % 2) + 256]
                        ve.wait_ge(o_ready, m + 1)
                        ve.scalar_tensor_tensor(out=part, in0=O_bank[:, 0:256], scalar=0.5, in1=part,
                                                op0=ALU.mult, op1=ALU.mult).then_inc(o_evac, 1)
                    if G_LN <= g < G_LN + ST:
                        layer_norm(g - G_LN)
                    h = g - 1
                    if h >= 0 and is_gate(h):
                        gate_ready(half, h)
                        if h < G_UA:
                            if half == 1 and h == G_Q + 1:
                                ve.wait_ge(y_stored, 16 * ST)
                            ve.scalar_tensor_tensor(out=mix[:, (h - G_Q) // 2, :], in0=act[:, 0:HS],
                                                    scalar=1.0, in1=pre[:, 0:HS], op0=ALU.add, op1=ALU.mult
                                                    ).then_inc(gate_used, 1)
                            ve.wait_ge(gate_used, GATES * half + gate_index(h) + 1)
                        elif h < G_GA:
                            j = h - G_UA
                            ve.wait_ge(sgu_ready, 4 * half + j + 1)
                            settle(ve.tensor_tensor(
                                aux[:, 0:HS].rearrange("p (b i) -> p b i", b=4),
                                E[0][:].rearrange("p (b i) -> p b i", b=4),
                                b_s_sb[:, j, :].unsqueeze(1).broadcast_to([P, 4, P]), ALU.add))
                            ve.tensor_tensor(mix[:, M_A + j, :], aux[:, 0:HS], act[:, 0:HS], ALU.mult
                                             ).then_inc(gate_used, 1)
                            ve.wait_ge(gate_used, GATES * half + gate_index(h) + 1)
                        elif h < G_C:
                            j = h - G_GA
                            ve.tensor_tensor(mix[:, M_A + j, :], mix[:, M_A + j, :], act[:, 0:HS], ALU.mult
                                             ).then_inc(gate_used, 1)
                        else:
                            j = (h - G_C) // 2
                            ve.wait_ge(pool_ready, 4 * half + j + 1)
                            ve.scalar_tensor_tensor(out=mix[:, M_C + j, :], in0=E[1][:],
                                                    scalar=c_scale_sb[:, j:j + 1], in1=act[:, 0:HS],
                                                    op0=ALU.mult, op1=ALU.mult).then_inc(gate_used, 1)
                    n = g - 1 - SLOT_S
                    if 0 <= n < PIECES:
                        softmax_norm(half, n)
                    if g == G_OUT - 1:
                        for kt in range(KT - 1):
                            mix_lo(half, kt)
                    if g == G_OUT:
                        mix_lo(half, KT - 1)
                    if half == 0 and g > G_LAST:
                        for kt in range(4 * (g - G_LAST - 1), 4 * (g - G_LAST)):
                            x_lo(1, kt)
            for st in range(2, ST):
                take_y(1, 3, (st,))
                finish_sum(st)
                finish(st)

        @block.tensor
        def _(pe):
            def w_tile(part, slot, at, n):
                return part[:, slot, at:at + n]

            def three(psum_out, stat, mov, first, last):
                pe.matmul(psum_out, stat[0], mov[0], start=first, stop=False)
                pe.matmul(psum_out, stat[0], mov[1], start=False, stop=False)
                return pe.matmul(psum_out, stat[1], mov[0], start=False, stop=last)

            def split_ready(G, part):
                pe.wait_ge(lo_done, split_index(G, part) + 1)

            def t_products(half, g, part):
                G = GROUPS * half + g
                bank = T[t_index(g) % 2]
                split_ready(G, part)
                n = KT // split_parts(G)
                for kt in range(n * part, n * part + n):
                    if g == 0:
                        pe.wait_ge(x_lo_done, KT * half + kt + 1)
                    at = P * kt
                    mm = three(bank[:], (w_tile(w_hi, G % 2, at, P), w_tile(w_lo, G % 2, at, P)),
                               (op_hi[:, kt, :], op_lo[:, kt, :]), kt == 0, kt == KT - 1)
                    if g == G_OUT - 1 and kt % 4 == 3 and kt < KT - 1:
                        mm.then_inc(x_read, 1)
                if part == split_parts(G) - 1:
                    mm.then_inc(group_done, 1)

            def t_free(half, g):
                n = T_TILES * half + t_index(g)
                if n >= 2:
                    pe.wait_ge(t_evac, n - 1)

            def k_tiles(half):
                t_free(half, 0)
                t_free(half, 1)
                for part in range(split_parts(GROUPS * half)):
                    for g in range(2):
                        t_products(half, g, part)

            def t_tile(half, g):
                t_free(half, g)
                for part in range(2):
                    t_products(half, g, part)

            def n_group(half, g, width, kts, sts=range(ST)):
                G = GROUPS * half + g
                for k, kt in enumerate(kts):
                    if k % (len(kts) // 2) == 0:
                        split_ready(G, k // (len(kts) // 2))
                    if g >= G_OUT and g < G_OUT + 4:
                        pe.wait_ge(m_lo_done, KT * half + kt + 1)
                    for st in sts:
                        pos = slice(P * st, P * st + P)
                        if kt == 0:
                            n_free(half, g, st)
                        mm = three(N[st][:, 0:width], (op_hi[:, kt, pos], op_lo[:, kt, pos]),
                                   (w_tile(w_hi, G % 2, width * k, width), w_tile(w_lo, G % 2, width * k, width)),
                                   kt == 0, kt == KT - 1)
                        if kt == KT - 1 and st != sts[-1]:
                            mm.then_inc(bank_done[st], 1)
                mm.then_inc(group_done, 1)

            def last_groups():
                g = GROUPS + 2
                for st in (2, 3):
                    for k in range(8):
                        G, kt, at = GROUPS + g + k // 4, 8 + k, 512 * (k % 4)
                        if k % 2 == 0:
                            split_ready(G, k % 4 // 2)
                        pos = slice(P * st, P * st + P)
                        mm = three(N[st][:], (op_hi[:, kt, pos], op_lo[:, kt, pos]),
                                   (w_tile(w_hi, G % 2, at, 512), w_tile(w_lo, G % 2, at, 512)), False, kt == KT - 1)
                        if st == 3 and k == 3:
                            mm.then_inc(group_done, 1)
                    if st == 2:
                        mm.then_inc(bank_done[st], 1)
                mm.then_inc(group_done, 1)

            def n_free(half, g, st):
                if g == G_V and half == 1:
                    pe.wait_ge(y_evac, ST * 3 + st + 1)
                if g == G_VA:
                    pe.wait_ge(v_evac, ST * half + st + 1)
                if g == G_OUT:
                    pe.wait_ge(o_evac, PIECES * (half + 1))
                if g > G_OUT:
                    c = min((g - G_OUT) // 4, 3)
                    pe.wait_ge(y_evac, ST * (4 * half + c - 1) + st + 1)

            def scores(half, n):
                i, tp, m = n // 2, n % 2, PIECES * half + n
                pe.wait_ge(q_lo_done, 16 * half + 2 * i + 2)
                if n == 0:
                    pe.wait_ge(k_lo_done, 8 * (half + 1))
                    pe.wait_ge(va_evac, ST * (half + 1))
                if m >= 1:
                    pe.wait_ge(shifted, 2 * m)
                for a in range(2):
                    for tl in range(2):
                        q0 = P * (2 * tp + tl)
                        for part in (k_hi, k_lo):
                            mm = pe.matmul(S_bank[a][:, WINDOW * tl:WINDOW * tl + WINDOW], q_stack[:, a, q0:q0 + P],
                                           part[:, 2 * (i // 4) + a, q0:q0 + WINDOW], start=part is k_hi,
                                           stop=part is k_lo)
                mm.then_inc(s_ready, 1)

            def transpose(half, n):
                m = PIECES * half + n
                pe.wait_ge(p_ready, m + 1)
                if m >= 1:
                    pe.wait_ge(pt_evac, m)
                for b in range(4):
                    mm = pe.transpose(PT_bank[:, P * b:P * b + P], probs[:, P * b:P * b + P], ident[:])
                mm.then_inc(pt_ready, 1)

            def values(half, n):
                i, tp, m = n // 2, n % 2, PIECES * half + n
                pe.wait_ge(pt_evac, m + 1)
                if m >= 1:
                    pe.wait_ge(o_evac, m)
                if n == 0:
                    pe.wait_ge(v_ready, 2 * (half + 1))
                for tl in range(2):
                    st = 2 * tp + tl
                    for a in range(2):
                        kv = 2 * (i // 4) + a
                        d, at = slice(64 * kv, 64 * kv + 64), (2 * a + tl) * P
                        for c, vals in enumerate((v_prev, v)):
                            mm = pe.matmul(O_bank[64 * a:64 * a + 64, P * tl + 64 * c:P * tl + 64 * c + 64],
                                           vals[:, st, d], probs_t[:, at + 64 * c:at + 64 * c + 64],
                                           start=True, stop=True)
                mm.then_inc(o_ready, 1)

            for half in range(HALVES):
                for g in range(GROUPS + 4 * half):
                    if g == 0:
                        k_tiles(half)
                    elif g == 1:
                        pass
                    elif is_t(g):
                        t_tile(half, g)
                    elif g < G_VA:
                        n_group(half, g, 256, range(8 * (g - G_V), 8 * (g - G_V) + 8))
                    elif g < G_Q:
                        n_group(half, g, 512, range(4 * (g - G_VA), 4 * (g - G_VA) + 4))
                    else:
                        k0 = 4 * ((g - G_OUT) % 4)
                        sts = range(ST)
                        if half == 1 and g >= G_LAST:
                            sts = range(2) if g < GROUPS else range(2, ST)
                        if g < GROUPS + 2:
                            n_group(half, g, 512, range(k0, k0 + 4), sts)
                        elif g == GROUPS + 2:
                            last_groups()
                    if g == 2:
                        pe.wait_ge(x_acc_done, (KT - 1) * (half + 1))
                        if half == 0:
                            pe.wait_ge(consts_set, 3)
                            pe.wait_ge(consts_loaded, 16 * 11)
                            pe.matmul(E[0][0:HEADS, 0:REL], rel_sb[:], one_hot_sb[:], start=True, stop=True)
                        pe.matmul(E[1][:], ones[:], rstd_row[:], start=True, stop=True)
                        for st in range(ST):
                            mm = pe.matmul(E[0][:, COLS + st:COLS + st + 1], rstd_row[:, P * st:P * st + P], ones[:, 0:1],
                                           start=True, stop=True)
                        mm.then_inc(stats_done, 1)
                    if 0 <= g - SLOT_PV < PIECES:
                        values(half, g - SLOT_PV)
                    if 0 <= g - SLOT_PT < PIECES:
                        transpose(half, g - SLOT_PT)
                    if 0 <= g - SLOT_S < PIECES:
                        scores(half, g - SLOT_S)
                    if G_UA <= g < G_GA:
                        j = g - G_UA
                        pe.wait_ge(ln_done, ST * (half + 1))
                        if j >= 1:
                            pe.wait_ge(gate_used, GATES * half + 8 + j)
                        for st in range(ST):
                            mm = pe.matmul(E[0][:, P * st:P * st + P], mix[:, M_A + j, P * st:P * st + P],
                                           w_s_sb[:, j, :], start=True, stop=True)
                        mm.then_inc(sgu_ready, 1)
                    if G_C <= g < G_OUT and g % 2 == 1:
                        j = (g - G_C) // 2
                        pe.wait_ge(pool_in, 4 * half + j + 1)
                        if j >= 1:
                            pe.wait_ge(gate_used, GATES * half + 16 + j)
                        pe.matmul(E[1][:], w_pool_sb[:, j, :], aux[:, HIST:HIST + HS], start=True, stop=True
                                  ).then_inc(pool_ready, 1)


def t5_bucket(rel):
    nb = REL_BUCKETS // 2
    exact = nb // 2
    n = np.abs(rel)
    large = exact + (np.log(np.maximum(n, 1).astype(np.float32) / exact)
                     / np.float32(math.log(REL_MAX_DIST / exact)) * (nb - exact)).astype(np.int32)
    return (rel > 0).astype(np.int32) * nb + np.where(n < exact, n, np.minimum(large, nb - 1))


def weight_stream(w_in, w_out):
    def tile(cols):
        return w_in[:, cols].reshape(KT, P, P).transpose(1, 0, 2).reshape(1, P, GW)

    def rows(m, at, width):
        part = m[:, at:at + width].reshape(KT, P, width).transpose(1, 0, 2)
        n = GW // width
        return part.reshape(P, KT // n, GW).transpose(1, 0, 2)

    span = lambda a, n: np.arange(a, a + n)
    pair = lambda base, i: np.concatenate([span(base + DH * h, DH) for h in tile_heads(i)])
    parts = [tile(span(2560 + P * p, P)) for p in range(2)]
    parts.append(rows(w_in, 2816, 256))
    parts.append(rows(w_in, 512, 512))
    for i in range(8):
        parts += [tile(pair(1536, i)), tile(pair(3072, i))]
    parts += [tile(span(P * j, P)) for j in range(4)]
    parts += [tile(span(1024 + P * j, P)) for j in range(4)]
    for j in range(4):
        parts += [tile(span(4096 + P * j, P)), tile(span(4608 + P * j, P))]
    order = np.concatenate([pair(512, i) for i in range(8)] + [span(0, 512), span(1536, 512)])
    mixed = w_out[order]
    parts += [rows(mixed, 512 * c, 512) for c in range(4)]
    return np.ascontiguousarray(np.concatenate(parts, axis=0))


def kernel(x, norm_g, w_in, a_ln_g, a_ln_b, a_w_s, a_b_s, b_sinks, rel_bias, c_w_pool, c_scale, w_out, final_g):
    import concourse.bacc as bacc
    from concourse.bass_utils import run_bass_kernel_spmd

    (x, norm_g, w_in, a_ln_g, a_ln_b, a_w_s, a_b_s, b_sinks, rel_bias, c_w_pool, c_scale, w_out, final_g) = (
        np.asarray(a) for a in (x, norm_g, w_in, a_ln_g, a_ln_b, a_w_s, a_b_s, b_sinks, rel_bias, c_w_pool,
                                c_scale, w_out, final_g))
    heads = np.array([h for i in range(8) for h in tile_heads(i)])
    one_hot = (t5_bucket(np.arange(REL) - 127)[None, :] == np.arange(REL_BUCKETS)[:, None]).astype(np.float32)
    counts = np.array([[1.0 / min(t + 1, window) for t in range(HIST)] for window in POOLS], np.float32)
    arrays = {
        "x": x[0],
        "x_t": x[0].T.reshape(4, 4, P, HALVES, HS).transpose(3, 0, 2, 1, 4).reshape(HALVES, 4, P, 4 * HS),
        "w": weight_stream(w_in[0], w_out[0]),
        "norm_g": norm_g[0].reshape(KT, P).T,
        "ln_g": a_ln_g, "ln_b": a_ln_b,
        "w_s": a_w_s[0].transpose(2, 0, 1).reshape(P, 4 * P),
        "b_s": a_b_s[0].reshape(1, 4 * P),
        "sinks": b_sinks[:, heads],
        "rel_bias": rel_bias[:, heads],
        "one_hot": one_hot,
        "inv_count": counts.reshape(1, 4 * HIST),
        "w_pool": c_w_pool[0].transpose(1, 0, 2).reshape(P, 4 * P),
        "c_scale": c_scale[0].reshape(4, P).T,
        "final_g": final_g.reshape(1, D),
    }
    arrays = {f"{k}_dram": np.ascontiguousarray(a) for k, a in arrays.items()}
    nc = bacc.Bacc("TRN2", target_bir_lowering=False, num_devices=1, dynamic_dma_scratch_size=1024)
    args = [nc.dram_tensor(k, a.shape, mybir.dt.from_np(a.dtype), kind="ExternalInput").ap()
            for k, a in arrays.items()]
    out = nc.dram_tensor("out_dram", (SEQ, D), F32, kind="ExternalOutput").ap()
    build(nc, *args, out)
    r = run_bass_kernel_spmd(nc, [arrays], core_ids=[0])
    return r.results[0]["out_dram"].reshape(1, SEQ, D)
```
